# Optimizing a Trainium2 kernel written in Bass

```python
import jax
import jax.numpy as jnp
from jax import lax
import numpy as np

D_MODEL = 2048
BATCH = 1
SEQ = 256
DEPTH = 2
DEC_BATCH = 8
DEC_SEQ = 8
PAST_LEN = 2048
PAGE_SIZE = 128

W_GLA = 3 * D_MODEL // 8
W_LRU = 3 * D_MODEL // 8
W_RET = D_MODEL - W_GLA - W_LRU
H_GLA = 4
DV_GLA = W_GLA // H_GLA
DK_GLA = DV_GLA // 2
GLA_RANK = 16
GLA_TAU = 16.0
H_LRU = 8
BLK_LRU = W_LRU // H_LRU
LRU_CONV = 4
LRU_C = 8.0
H_RET = 4
DK_RET = W_RET // H_RET
DV_RET = W_RET // H_RET
ROPE_BASE = 10000.0
D_FF = 5632
FFN_CONV = 3
CHUNK = 64
EPS = 1e-6
IN_SIZES = (H_GLA * DK_GLA, H_GLA * DK_GLA, W_GLA, GLA_RANK, W_GLA, W_LRU, W_LRU, W_RET, W_RET, W_RET, W_RET)
N_IN = sum(IN_SIZES)

kernel_name = "hymba_gla_rglru_retention_convffn_step"

def _rmsnorm(x, g):
    xf = x.astype(jnp.float32)
    y = xf * lax.rsqrt(jnp.mean(xf * xf, axis=-1, keepdims=True) + EPS)
    return y.astype(x.dtype) * g

def _head_rmsnorm(o, g):
    y = o * lax.rsqrt(jnp.mean(o * o, axis=-1, keepdims=True) + EPS)
    B, T, H, Dv = o.shape
    return y.reshape(B, T, H * Dv) * g.astype(jnp.float32)

def _split_cols(z, sizes):
    outs = []
    off = 0
    for s in sizes:
        outs.append(z[..., off:off + s])
        off += s
    return outs

def _causal_dwconv(x, buf, w, b):
    K = w.shape[0]
    T = x.shape[1]
    xe = jnp.concatenate([buf.astype(x.dtype), x], axis=1)
    y = xe[:, 0:T] * w[0] + b
    for k in range(1, K):
        y = y + xe[:, k:k + T] * w[k]
    return y, xe[:, T:]

def _chunk_len(T):
    return CHUNK if T % CHUNK == 0 else T

def _to_chunks(a, C):
    B, T, H, X = a.shape
    return a.reshape(B, T // C, C, H, X).transpose(1, 0, 3, 2, 4)

def _from_chunks(a):
    N, B, H, C, X = a.shape
    return a.transpose(1, 0, 3, 2, 4).reshape(B, N * C, H, X)

def _rope(x, pos):
    half = x.shape[-1] // 2
    freqs = ROPE_BASE ** (-jnp.arange(half, dtype=jnp.float32) / half)
    ang = pos.astype(jnp.float32)[:, None] * freqs[None, :]
    cos = jnp.cos(ang)[None, :, None, :]
    sin = jnp.sin(ang)[None, :, None, :]
    x1 = x[..., :half].astype(jnp.float32)
    x2 = x[..., half:].astype(jnp.float32)
    return jnp.concatenate([x1 * cos - x2 * sin, x1 * sin + x2 * cos], axis=-1).astype(x.dtype)

def _gla(q, k, v, log_a, S0):
    T = q.shape[1]
    C = _chunk_len(T)
    f32 = jnp.float32
    causal = jnp.tril(jnp.ones((C, C), dtype=bool))[:, :, None]

    def step(S, inp):
        qc, kc, vc, ac = inp
        b = jnp.cumsum(ac, axis=2)
        diff = b[:, :, :, None, :] - b[:, :, None, :, :]
        decay = jnp.exp(jnp.where(causal, diff, -jnp.inf))
        att = jnp.einsum('bhtd,bhsd,bhtsd->bhts', qc, kc, decay)
        o = jnp.einsum('bhts,bhsv->bhtv', att, vc) + jnp.einsum('bhtd,bhdv->bhtv', qc * jnp.exp(b), S)
        b_last = b[:, :, -1:, :]
        S = jnp.exp(b_last[:, :, 0, :])[..., None] * S + jnp.einsum('bhsd,bhsv->bhdv', kc * jnp.exp(b_last - b), vc)
        return S, o

    xs = (_to_chunks(q.astype(f32), C), _to_chunks(k.astype(f32), C), _to_chunks(v.astype(f32), C), _to_chunks(log_a.astype(f32), C))
    S, o = lax.scan(step, S0.astype(f32), xs)
    return _from_chunks(o), S.astype(S0.dtype)

def _retention(q, k, v, S0):
    T = q.shape[1]
    H = q.shape[2]
    C = _chunk_len(T)
    f32 = jnp.float32
    log_g = jnp.log1p(-jnp.exp2(-5.0 - jnp.arange(H, dtype=f32)))
    idx = jnp.arange(C, dtype=f32)
    rel = idx[:, None] - idx[None, :]
    decay_in = jnp.where(rel[None] >= 0, jnp.exp(jnp.maximum(rel, 0.0)[None] * log_g[:, None, None]), 0.0)
    q_dec = jnp.exp((idx + 1.0)[None, :] * log_g[:, None])[None, :, :, None]
    k_dec = jnp.exp((C - 1.0 - idx)[None, :] * log_g[:, None])[None, :, :, None]
    c_dec = jnp.exp(C * log_g)[None, :, None, None]

    def step(S, inp):
        qc, kc, vc = inp
        att = jnp.einsum('bhtd,bhsd->bhts', qc, kc) * decay_in[None]
        o = jnp.einsum('bhts,bhsv->bhtv', att, vc) + jnp.einsum('bhtd,bhdv->bhtv', qc, S) * q_dec
        S = c_dec * S + jnp.einsum('bhsd,bhsv->bhdv', kc * k_dec, vc)
        return S, o

    xs = (_to_chunks(q.astype(f32), C), _to_chunks(k.astype(f32), C), _to_chunks(v.astype(f32), C))
    S, o = lax.scan(step, S0.astype(f32), xs)
    return _from_chunks(o), S.astype(S0.dtype)

def _lin_combine(left, right):
    a1, b1 = left
    a2, b2 = right
    return a1 * a2, a2 * b1 + b2

def _rglru(xc, h0, w_a, b_a, w_x, b_x, lam):
    B, T, W = xc.shape
    f32 = jnp.float32
    xf = xc.astype(f32)
    xb = xf.reshape(B, T, H_LRU, W // H_LRU)
    r = jax.nn.sigmoid(jnp.einsum('bthi,hij->bthj', xb, w_a.astype(f32)).reshape(B, T, W) + b_a.astype(f32))
    i = jax.nn.sigmoid(jnp.einsum('bthi,hij->bthj', xb, w_x.astype(f32)).reshape(B, T, W) + b_x.astype(f32))
    log_a = -LRU_C * r * jax.nn.softplus(-lam.astype(f32))
    a = jnp.exp(log_a)
    u = jnp.sqrt(-jnp.expm1(2.0 * log_a)) * (i * xf)
    u = u.at[:, 0].add(a[:, 0] * h0.astype(f32))
    _, h = lax.associative_scan(_lin_combine, (a, u), axis=1)
    return h, h[:, -1].astype(h0.dtype)

def _token_mixers(hn, pos, S_gla, S_ret, h_lru, buf_lru, w_in, gla_w_alpha, gla_b_alpha, gla_norm_g,
                  lru_conv_w, lru_conv_b, lru_w_a, lru_b_a, lru_w_x, lru_b_x, lru_lambda, ret_norm_g, w_out):
    B, T, _ = hn.shape
    f32 = jnp.float32
    z = hn @ w_in
    gq, gk, gv, g_lr, g_gate, l_x, l_gate, rq, rk, rv, r_gate = _split_cols(z, IN_SIZES)
    q = gq.reshape(B, T, H_GLA, DK_GLA) * (DK_GLA ** -0.5)
    k = gk.reshape(B, T, H_GLA, DK_GLA)
    v = gv.reshape(B, T, H_GLA, DV_GLA)
    log_a = jax.nn.log_sigmoid((g_lr @ gla_w_alpha + gla_b_alpha).astype(f32)) / GLA_TAU
    o, S_gla = _gla(q, k, v, log_a.reshape(B, T, H_GLA, DK_GLA), S_gla)
    o_gla = _head_rmsnorm(o, gla_norm_g) * jax.nn.silu(g_gate.astype(f32))
    xc, buf_lru = _causal_dwconv(l_x, buf_lru, lru_conv_w, lru_conv_b)
    h, h_lru = _rglru(xc, h_lru, lru_w_a, lru_b_a, lru_w_x, lru_b_x, lru_lambda)
    o_lru = h * jax.nn.gelu(l_gate.astype(f32))
    q = _rope(rq.reshape(B, T, H_RET, DK_RET), pos) * (DK_RET ** -0.5)
    k = _rope(rk.reshape(B, T, H_RET, DK_RET), pos)
    v = rv.reshape(B, T, H_RET, DV_RET)
    o, S_ret = _retention(q, k, v, S_ret)
    o_ret = _head_rmsnorm(o, ret_norm_g) * jax.nn.silu(r_gate.astype(f32))
    mixed = jnp.concatenate([o_gla, o_lru, o_ret], axis=-1).astype(hn.dtype)
    return mixed @ w_out, S_gla, S_ret, h_lru, buf_lru

def _conv_ffn(hn, buf, w_up, conv_w, conv_b, w_down):
    up = hn @ w_up
    u, buf = _causal_dwconv(up, buf, conv_w, conv_b)
    gate = u[..., :D_FF]
    val = u[..., D_FF:]
    return (jax.nn.silu(gate) * val) @ w_down, buf

def _run_group(x, c, start, st_gla, st_ret, st_lru, st_lru_conv, st_ffn_conv,
               norm1_g, norm2_g, final_g, w_ada, b_ada, w_in, gla_w_alpha, gla_b_alpha, gla_norm_g,
               lru_conv_w, lru_conv_b, lru_w_a, lru_b_a, lru_w_x, lru_b_x, lru_lambda, ret_norm_g, w_out,
               ffn_w_up, ffn_conv_w, ffn_conv_b, ffn_w_down):
    T = x.shape[1]
    pos = start + jnp.arange(T, dtype=jnp.int32)
    n_gla, n_ret, n_lru, n_lconv, n_fconv = [], [], [], [], []
    c_act = jax.nn.silu(c)
    for l in range(DEPTH):
        mod = c_act @ w_ada[l] + b_ada[l]
        sh1, sc1, g1, sh2, sc2, g2 = jnp.split(mod, 6, axis=-1)
        hn = _rmsnorm(x, norm1_g[l]) * (1 + sc1[:, None]) + sh1[:, None]
        m, S_gla, S_ret, h_lru, b_lru = _token_mixers(
            hn, pos, st_gla[l], st_ret[l], st_lru[l], st_lru_conv[l], w_in[l], gla_w_alpha[l], gla_b_alpha[l],
            gla_norm_g[l], lru_conv_w[l], lru_conv_b[l], lru_w_a[l], lru_b_a[l], lru_w_x[l], lru_b_x[l],
            lru_lambda[l], ret_norm_g[l], w_out[l])
        x = x + g1[:, None] * m
        hn = _rmsnorm(x, norm2_g[l]) * (1 + sc2[:, None]) + sh2[:, None]
        f, b_ffn = _conv_ffn(hn, st_ffn_conv[l], ffn_w_up[l], ffn_conv_w[l], ffn_conv_b[l], ffn_w_down[l])
        x = x + g2[:, None] * f
        n_gla.append(S_gla)
        n_ret.append(S_ret)
        n_lru.append(h_lru)
        n_lconv.append(b_lru)
        n_fconv.append(b_ffn)
    y = _rmsnorm(x, final_g)
    return y, jnp.stack(n_gla), jnp.stack(n_ret), jnp.stack(n_lru), jnp.stack(n_lconv), jnp.stack(n_fconv)

def setup_inputs(seed: int = 0) -> dict:
    key = jax.random.key(seed)
    ks = jax.random.split(key, 32)
    f32 = jnp.float32
    D = D_MODEL

    def nrm(k, shape, scale):
        return jax.random.normal(k, shape, f32) * scale

    a_c = jax.random.uniform(ks[24], (DEPTH, W_LRU), f32, 0.9, 0.999)
    a0 = a_c ** (1.0 / LRU_C)
    return {
        'x_prompt': nrm(ks[0], (BATCH, SEQ, D), 1.0),
        'x_sample': nrm(ks[1], (DEC_BATCH, DEC_SEQ, D), 1.0),
        'state_gla': nrm(ks[2], (DEPTH, DEC_BATCH, H_GLA, DK_GLA, DV_GLA), 1.0),
        'state_ret': nrm(ks[3], (DEPTH, DEC_BATCH, H_RET, DK_RET, DV_RET), 1.0),
        'state_lru': nrm(ks[4], (DEPTH, DEC_BATCH, W_LRU), 0.5),
        'state_lru_conv': nrm(ks[5], (DEPTH, DEC_BATCH, LRU_CONV - 1, W_LRU), 1.0),
        'state_ffn_conv': nrm(ks[6], (DEPTH, DEC_BATCH, FFN_CONV - 1, 2 * D_FF), 1.0),
        'c_prompt': nrm(ks[7], (BATCH, D), 1.0),
        'c_sample': nrm(ks[8], (DEC_BATCH, D), 1.0),
        'norm1_g': 1.0 + nrm(ks[9], (DEPTH, D), 0.02),
        'norm2_g': 1.0 + nrm(ks[10], (DEPTH, D), 0.02),
        'final_g': 1.0 + nrm(ks[11], (D,), 0.02),
        'w_ada': nrm(ks[12], (DEPTH, D, 6 * D), 0.5 * D ** -0.5),
        'b_ada': nrm(ks[13], (DEPTH, 6 * D), 0.02),
        'w_in': nrm(ks[14], (DEPTH, D, N_IN), D ** -0.5),
        'gla_w_alpha': nrm(ks[15], (DEPTH, GLA_RANK, H_GLA * DK_GLA), GLA_RANK ** -0.5),
        'gla_b_alpha': nrm(ks[16], (DEPTH, H_GLA * DK_GLA), 0.1),
        'gla_norm_g': 1.0 + nrm(ks[17], (DEPTH, W_GLA), 0.02),
        'lru_conv_w': nrm(ks[18], (DEPTH, LRU_CONV, W_LRU), LRU_CONV ** -0.5),
        'lru_conv_b': nrm(ks[19], (DEPTH, W_LRU), 0.02),
        'lru_w_a': nrm(ks[20], (DEPTH, H_LRU, BLK_LRU, BLK_LRU), BLK_LRU ** -0.5),
        'lru_b_a': nrm(ks[21], (DEPTH, W_LRU), 0.1),
        'lru_w_x': nrm(ks[22], (DEPTH, H_LRU, BLK_LRU, BLK_LRU), BLK_LRU ** -0.5),
        'lru_b_x': nrm(ks[23], (DEPTH, W_LRU), 0.1),
        'lru_lambda': jnp.log(a0) - jnp.log1p(-a0),
        'ret_norm_g': 1.0 + nrm(ks[25], (DEPTH, W_RET), 0.02),
        'w_out': nrm(ks[26], (DEPTH, D, D), D ** -0.5),
        'ffn_w_up': nrm(ks[27], (DEPTH, D, 2 * D_FF), D ** -0.5),
        'ffn_conv_w': nrm(ks[28], (DEPTH, FFN_CONV, 2 * D_FF), FFN_CONV ** -0.5),
        'ffn_conv_b': nrm(ks[29], (DEPTH, 2 * D_FF), 0.02),
        'ffn_w_down': nrm(ks[30], (DEPTH, D_FF, D), D_FF ** -0.5),
    }

def reference(x_prompt, x_sample, state_gla, state_ret, state_lru, state_lru_conv, state_ffn_conv,
              c_prompt, c_sample, norm1_g, norm2_g, final_g, w_ada, b_ada, w_in, gla_w_alpha, gla_b_alpha,
              gla_norm_g, lru_conv_w, lru_conv_b, lru_w_a, lru_b_a, lru_w_x, lru_b_x, lru_lambda, ret_norm_g,
              w_out, ffn_w_up, ffn_conv_w, ffn_conv_b, ffn_w_down):
    B = x_prompt.shape[0]
    dt = x_prompt.dtype
    z_gla = jnp.zeros((DEPTH, B, H_GLA, DK_GLA, DV_GLA), dt)
    z_ret = jnp.zeros((DEPTH, B, H_RET, DK_RET, DV_RET), dt)
    z_lru = jnp.zeros((DEPTH, B, W_LRU), dt)
    z_lconv = jnp.zeros((DEPTH, B, LRU_CONV - 1, W_LRU), dt)
    z_fconv = jnp.zeros((DEPTH, B, FFN_CONV - 1, 2 * D_FF), dt)
    y_prompt, p_gla, p_ret, p_lru, p_lconv, p_fconv = _run_group(
        x_prompt, c_prompt, 0, z_gla, z_ret, z_lru, z_lconv, z_fconv,
        norm1_g, norm2_g, final_g, w_ada, b_ada, w_in, gla_w_alpha, gla_b_alpha, gla_norm_g,
        lru_conv_w, lru_conv_b, lru_w_a, lru_b_a, lru_w_x, lru_b_x, lru_lambda, ret_norm_g, w_out,
        ffn_w_up, ffn_conv_w, ffn_conv_b, ffn_w_down)
    y_sample, s_gla, s_ret, s_lru, s_lconv, s_fconv = _run_group(
        x_sample, c_sample, PAST_LEN, state_gla, state_ret, state_lru, state_lru_conv, state_ffn_conv,
        norm1_g, norm2_g, final_g, w_ada, b_ada, w_in, gla_w_alpha, gla_b_alpha, gla_norm_g,
        lru_conv_w, lru_conv_b, lru_w_a, lru_b_a, lru_w_x, lru_b_x, lru_lambda, ret_norm_g, w_out,
        ffn_w_up, ffn_conv_w, ffn_conv_b, ffn_w_down)
    return (y_prompt, y_sample, p_gla, p_ret, p_lru, p_lconv, p_fconv, s_gla, s_ret, s_lru, s_lconv, s_fconv)


_drawn_inputs = setup_inputs


def setup_inputs(seed=0):
    import zlib

    import numpy as np

    out = dict(_drawn_inputs(seed))
    spreads = {}
    factors = {'norm2_g': 2.883,
     'final_g': 2.901,
     'gla_norm_g': 8.0,
     'lru_b_a': 3.601,
     'ret_norm_g': 8.0,
     'ffn_conv_b': 7.334}
    for name, (base, spread) in spreads.items():
        noise = np.random.default_rng([zlib.crc32(name.encode()), seed]).standard_normal(out[name].shape)
        drawn = base * np.exp(spread * noise) if base else spread * noise
        out[name] = jnp.asarray(drawn.astype(out[name].dtype))
    for name, factor in factors.items():
        out[name] = (out[name] * factor).astype(out[name].dtype)
    return out
```

```python
import concourse.bass as bass
from concourse import mybir
from concourse.alu_op_type import AluOpType as ALU
from contextlib import ExitStack
import math

D = 2048
DEPTH = 2
SEQ = 256
NS, TS = 8, 8
T = SEQ + NS * TS
W3 = 768
WR = 512
H = 4
DK, DV = 96, 192
DR = 128
RANK = 16
N_IN = 5904
D_FF = 5632
P = 128
KC = D // P
NB_FF = 2 * D_FF // P
EPS = 1e-6
QSCALE = DK ** -0.5
SP = slice(0, SEQ)
SS = slice(SEQ, T)

ADA_PANELS = 6 * D // 256
ADA_UNITS = 4 * ADA_PANELS
ADA_FIRST = ADA_PANELS // 3
ADA_LATE = 4 * (ADA_PANELS - ADA_FIRST)
W_IN_UNITS = 4 * 25
PARTS = (8, 8, 6)
DOWN_K = (4, 4, 3)
MAIN_UNITS = W_IN_UNITS + 32 + sum(8 * n for n in PARTS) + sum(8 * k for k in DOWN_K)
UNITS = ADA_UNITS + MAIN_UNITS
GRANULES = 2 * MAIN_UNITS
LATE_AT = W_IN_UNITS + 2
PANELS = ADA_PANELS + 24 + 8 + 2 * sum(PARTS) + 24
LOOK = 4

G_QK, G_V, G_GLR, G_REST = 0, 32, 64, 72
G_OUT = 200
G_UP, G_DOWN = [], []
_g = G_OUT + 64
for _n, _k in zip(PARTS, DOWN_K):
    G_UP.append(_g)
    _g += 16 * _n
    G_DOWN.append(_g)
    _g += 16 * _k
assert _g == GRANULES

C_N1, C_N2, C_BADA = 0, 16, 32
C_GN, C_CW, C_CB, C_BA, C_BX, C_LAM, C_RN, C_FG, C_AL = 128, 134, 158, 164, 170, 176, 182, 186, 202
C_FF = 256
SH1, SC1, GA1, SH2, SC2, GA2 = (16 * i for i in range(6))

LEVELS = (64, 32, 16, 8, 4, 2, 1, 0)


def gla_segments(h):
    if h % 2 == 0:
        return [(h // 2 * 3, 0, 128, 0), (h // 2 * 3 + 1, 0, 64, 128)]
    return [(h // 2 * 3 + 1, 64, 64, 0), (h // 2 * 3 + 2, 0, 128, 64)]


def psum_jobs():
    pro = ["c"] + [f"x{t}_{k}" for t in range(3) for k in range(4)]
    lay = [f"par{i}" for i in range(7)] + ["ss1", "mod0", "glr"]
    lay += [f"alpha{h}" for h in range(H)] + [f"vt{t}_{k}" for t in range(3) for k in range(2)]
    for h in range(H):
        lay += [f"lev{h}_{i}" for i in range(8)] + [f"kt{h}", f"kv{h}_0", f"o{h}_0", f"o{h}_1", f"kv{h}_1"]
        lay += [f"kvs{h}_{i}" for i in range(4)]
    lay += ["hs"] + [f"bc{j}" for j in range(6)]
    lay += ["lcv", "lco0", "lco1"] + [f"gate{g}_{j}" for j in range(6) for g in range(2)] + ["lho0", "lho1"]
    lay += [f"rvt{t}" for t in range(3)]
    for h in range(H):
        lay += [f"rqk{h}", f"rkt{h}", f"rkv{h}_0", f"ro{h}", f"rkv{h}_1", f"rkvs{h}_0", f"rkvs{h}_1"]
    lay += ["rhs"] + [f"rbc{j}" for j in range(4)]
    lay += ["mod1", "mod2"]
    lay += [f"hist{j}" for j in range(22)] + ["ss2"] + [f"xo{j}" for j in range(22)]
    epi = ["ssf"] + [f"y{t}_{k}" for t in range(3) for k in range(4)]
    table, per_bank = {}, [[0] * 4, [0] * 4, [0] * 4]
    for part, names in enumerate((pro, lay, epi)):
        for i, name in enumerate(names):
            b = i % 4
            table[name] = (part, i, b, per_bank[part][b])
            per_bank[part][b] += 1
    return table, [len(pro), len(lay)], per_bank


def late_units(names):
    first = list(names).index("alpha0") + 1
    return {name: v for v, name in enumerate(list(names)[first:first + ADA_LATE])}


def build(nc, I, O):
    f32, f32r, u8 = mybir.dt.float32, mybir.dt.float32r, mybir.dt.uint8
    ACT = mybir.ActivationFunctionType
    JOB, NJOB, NBANK = psum_jobs()
    LATE = late_units(JOB)
    assert JOB["mod1"][1] > JOB[list(LATE)[-1]][1]

    ctx = ExitStack()
    with ctx:
        base = (nc.sbuf_base + 31) // 32 * 32
        spot = [base]

        def at(name, shape, dt, offset):
            return nc.alloc_sbuf_tensor_at(name, shape, dt, offset=offset)

        def new(name, shape, dt):
            size = math.prod(shape[1:]) * (1 if dt == u8 else 4)
            t = at(name, shape, dt, spot[0])
            spot[0] += (size + 31) // 32 * 32
            return t

        X = new("X", [P, KC, T], f32)
        HH = new("HH", [P, KC, T], f32r)
        HL = new("HL", [P, KC, T], f32r)
        m_at = spot[0]
        MH = new("MH", [P, KC, T], f32r)
        ML = new("ML", [P, KC, T], f32r)
        RAW = new("RAW", [P, 4, 4, 256], f32)
        WHI = new("WHI", [P, 4, 2, 256], f32r)
        WLO = new("WLO", [P, 4, 2, 256], f32r)
        z_at = spot[0]
        Z = new("Z", [P, 48, T], f32)
        CST = new("CST", [P, 304], f32)
        PAR = new("PAR", [P, 608], f32)
        MOD = new("MOD", [P, 96, 9], f32)
        CACT = new("CACT", [P, KC, 9], f32)
        RS = new("RS", [P, T], f32)
        TMP = new("TMP", [P, 2, T], f32)
        WAL = new("WAL", [RANK, H * DK], f32)
        KEEP = new("KEEP", [P, T], f32)
        GS = new("GS", [P, 2, 9], f32)
        EB = new("EB", [DK, 2, 10], f32)
        C8 = new("C8", [P, 3, 6], f32)
        CW = new("CW", [P, 2, 4, 2], f32)
        assert spot[0] <= nc.sbuf_usable_end, (spot[0], nc.sbuf_usable_end)

        IDENT, ONES = CST[:, 0:128], CST[:, 128:256]
        HIND = CST[:, 256:280].rearrange("p (t h) -> p t h", h=4)
        RIND = CST[:, 280:296].rearrange("p (t h) -> p t h", h=4)
        SEL = CST[0:64, 296:304]

        BLK = T * 4
        STG = at("STG", [P, 7, 128], f32, z_at + 16 * BLK)
        XIN = at("XIN", [P, 3, D], f32, z_at + 8 * BLK)
        CIN = at("CIN", [9, D], f32, z_at + 28 * BLK)
        SQ = at("SQ", [P, KC, T], f32, m_at - KC * BLK)
        NT = at("NT", [P, 6, T], f32, z_at + 8 * BLK)
        ROWS = at("ROWS", [9, ADA_LATE // 4 * 256], f32, m_at - 2 * KC * BLK)
        assert ADA_LATE // 4 * 256 * 4 <= 2 * KC * BLK
        VTM = at("VTM", [P, 3, W3], f32, m_at)
        MSK = at("MSK", [P, 8, 192], f32, m_at)
        BC = at("BC", [DK, H, T], f32, m_at + 9216)
        DE = at("DE", [DK, H, T], f32, m_at + 14336)
        QP = at("QP", [DK, 2, T], f32, m_at + 19456)
        KP = at("KP", [DK, 2, T], f32, m_at + 22016)
        LA2 = at("LA2", [DK, H, T], f32, m_at + 19456)
        ATT = at("ATT", [P, 2, T], f32, m_at + 24576)
        ST = at("ST", [DK, 10, DV], f32, m_at + 27136)
        KTM = at("KTM", [P, 3, DK], f32, m_at + 34816)
        KTMM = at("KTMM", [64, NS, DK], f32, m_at + 35968)
        GM = at("GM", [P, 8, 192], u8, m_at + 39040)
        assert 39040 + 1536 <= 2 * KC * BLK
        XE = at("XE", [P, 6, 347], f32, z_at)
        XC = at("XC", [P, 6, T], f32, z_at + 7 * BLK)
        GR = at("GR", [P, 6, T], f32, z_at + 13 * BLK)
        GI = at("GI", [P, 6, T], f32, z_at + 20 * BLK)
        AA = at("AA", [P, 6, T], f32, z_at)
        H0 = at("H0", [P, 6, 8], f32, z_at + 19 * BLK)
        U0 = at("U0", [P, 6, 8], f32, z_at + 19 * BLK + 192)
        LCO = at("LCO", [P, 6, 27], f32, z_at + 19 * BLK + 384)
        LHO = at("LHO", [P, 6, 9], f32, z_at + 19 * BLK + 1056)
        mh6, ml6 = m_at + 6 * BLK, m_at + (KC + 6) * BLK
        GW = [at("GWA", [P, 6, 192], f32, m_at + 12 * BLK), at("GWX", [P, 6, 192], f32, m_at + (KC + 12) * BLK)]
        SLC = at("SLC", [24, W3], f32, ml6)
        OLC = at("OLC", [27, W3], f32, ml6 + 3072)
        SLH = at("SLH", [8, W3], f32, mh6)
        OLH = at("OLH", [9, W3], f32, mh6 + 3072)
        COS = at("COS", [P, T], f32, z_at)
        SIN = at("SIN", [P, T], f32, z_at + BLK)
        RD = at("RD", [P, H, 192], f32, z_at + 2 * BLK)
        QD = at("QD", [P, H, T], f32, z_at + 5 * BLK)
        KD = at("KD", [P, 2, H], f32, z_at + 4 * BLK + 512)
        ROT = at("ROT", [P, H, T], f32, z_at + 9 * BLK)
        RVT = at("RVT", [P, 3, WR], f32, z_at + 13 * BLK)
        RAT = at("RAT", [P, 2, T], f32, z_at + 18 * BLK)
        RKT = at("RKT", [P, 3, DR], f32, z_at + 20 * BLK)
        RKM = at("RKM", [64, NS, DR], f32, z_at + 22 * BLK)
        RST = at("RST", [P, 10, DR], f32, z_at + 26 * BLK)
        RQE = at("RQE", [P, 2, T], f32, z_at + 30 * BLK)
        STF = at("STF", [16, 2 * D_FF], f32, z_at)
        HIST = at("HIST", [P, NB_FF, 16], f32, z_at + 36 * BLK)
        XO = at("XO", [P, NB_FF, 18], f32, z_at + 41 * BLK)
        EXT = at("EXT", [P, 4, 338], f32, z_at)
        YC = at("YC", [P, 4, 338], f32, z_at + 5 * BLK)
        HF = at("HF", [P, 2, T], f32, z_at + 10 * BLK)
        OUTF = at("OUTF", [18, 2, 512], f32, z_at + 12 * BLK)
        YO = at("YO", [P, 3, D], f32, m_at)

        PS = ctx.enter_context(nc.psum_tensor("PS", [P, 8, 512], f32))

        def sem(name):
            return ctx.enter_context(nc.semaphore(name))

        raw_loaded = [sem(f"raw_loaded{i}") for i in range(4)]
        ada_used = sem("ada_used")
        rows_mod = sem("rows_mod")
        hi_ready = sem("hi_ready")
        split_ready = sem("split_ready")
        split_used = sem("split_used")
        pair_free = [sem("pair_free0"), sem("pair_free1")]
        job_done = sem("job_done")
        bank_free = [sem(f"bank_free{i}") for i in range(4)]
        consts_in = sem("consts_in")
        inputs_in = sem("inputs_in")
        credits = sem("credits")
        turns = sem("turns")
        picks = sem("picks")
        x_ready = sem("x_ready")
        c_ready = sem("c_ready")
        params_in = sem("params_in")
        par_ready = sem("par_ready")
        sq_ready = sem("sq_ready")
        stage_free = sem("stage_free")
        ms_ready = sem("ms_ready")
        rms_ready = sem("rms_ready")
        rs_ready = sem("rs_ready")
        hn_f32 = sem("hn_f32")
        hn_hi = sem("hn_hi")
        hn_ready = sem("hn_ready")
        glr_ready = sem("glr_ready")
        z_ready = sem("z_ready")
        masks_in = sem("masks_in")
        masks_ready = sem("masks_ready")
        q_scaled = sem("q_scaled")
        alpha_in = sem("alpha_in")
        softp = sem("softp")
        b_ready = sem("b_ready")
        v_ready = sem("v_ready")
        diff_ready = sem("diff_ready")
        decay_ready = sem("decay_ready")
        qk_ready = sem("qk_ready")
        ktm_ready = sem("ktm_ready")
        ktmm_ready = sem("ktmm_ready")
        s1_ready = sem("s1_ready")
        att_ready = sem("att_ready")
        o_ready = sem("o_ready")
        state_in = sem("state_in")
        state_new = sem("state_new")
        state_out = sem("state_out")
        osq_ready = sem("osq_ready")
        hms_ready = sem("hms_ready")
        hrms_ready = sem("hrms_ready")
        hrs_ready = sem("hrs_ready")
        gates_ready = sem("gates_ready")
        mix_f32 = sem("mix_f32")
        mix_hi = sem("mix_hi")
        mix_ready = sem("mix_ready")
        gw_zero = sem("gw_zero")
        lru_in = sem("lru_in")
        xe_ready = sem("xe_ready")
        xc_ready = sem("xc_ready")
        lco_ready = sem("lco_ready")
        ri_ready = sem("ri_ready")
        la_ready = sem("la_ready")
        a_ready = sem("a_ready")
        em_ready = sem("em_ready")
        root_ready = sem("root_ready")
        lho_ready = sem("lho_ready")
        lru_rows = sem("lru_rows")
        lru_out = sem("lru_out")
        rtab_in = sem("rtab_in")
        rot_ready = sem("rot_ready")
        rope_done = sem("rope_done")
        hist_in = sem("hist_in")
        hist_ready = sem("hist_ready")
        x_mid = sem("x_mid")
        x_new = sem("x_new")
        ext_ready = sem("ext_ready")
        conv_done = sem("conv_done")
        silu_done = sem("silu_done")
        hid_f32 = sem("hid_f32")
        hid_hi = sem("hid_hi")
        hid_ready = sem("hid_ready")
        rows_out = [sem("rows_out0"), sem("rows_out1")]
        y_rows = sem("y_rows")
        y_out = sem("y_out")

        block = ctx.enter_context(nc.Block())

        def job_value(name, l):
            part, i, _, _ = JOB[name]
            return i + 1 if part == 0 else NJOB[0] + (l * NJOB[1] if part == 1 else DEPTH * NJOB[1]) + i + 1

        def bank_value(name, l):
            part, _, b, i = JOB[name]
            return i + 1 if part == 0 else NBANK[0][b] + (l * NBANK[1][b] if part == 1 else DEPTH * NBANK[1][b]) + i + 1

        def bank(name):
            return PS[:, 4 + JOB[name][2], :]

        def freed(name):
            return bank_free[JOB[name][2]]

        def loaded(l, rounds, g):
            u = g // 2
            pos = 4 * ADA_FIRST + u + (ADA_LATE if u >= LATE_AT else 0)
            return u % 4, g % 2 * 2, (l * (UNITS // 4) + rounds + (pos // 4 + 1)) * 16

        def panel_used(l, g_end):
            return l * GRANULES + g_end + LOOK

        def last_granules(q):
            a, b = (min(6 * i + LOOK, 48) for i in (q, q + 1))
            a = a + 4 if q == 0 else a
            return G_DOWN[2] + a, b - a

        def pair_value(l, k):
            return l * (PANELS // 2) + k + 1

        Q_QK = ADA_FIRST
        Q_V = Q_QK + 4
        Q_REST = Q_V + 4
        Q_LATE = Q_REST + 16
        Q_OUT = Q_LATE + ADA_LATE // 4
        Q_UP, Q_DOWN, q = [], [], Q_OUT + 8
        for n in PARTS:
            Q_UP.append(q)
            Q_DOWN.append(q + 2 * n)
            q += 2 * n + 8
        assert q == PANELS

        tiles = [(slice(0, 128), 128), (slice(128, 256), 128), (slice(256, 320), 64)]

        def rows2(ap):
            return ap.rearrange("l k n -> (l k) n")

        w_ada, w_in, w_out = rows2(I["w_ada"]), rows2(I["w_in"]), rows2(I["w_out"])
        w_up, w_down = rows2(I["ffn_w_up"]), rows2(I["ffn_w_down"])

        @block.sync
        def _(sp):
            def load(s, src, width=256):
                sp.dma_start(RAW[:, s, :, 0:width], src).then_inc(raw_loaded[s], 16)

            def unit(l, m, s, src, width=256):
                sp.wait_ge(split_ready, l * GRANULES + 2 * m + 2)
                load(s, src, width)

            def block_of(w, row, col, width=256):
                return w[bass.ds(row, 512), bass.ds(col, width)].rearrange("(c p) n -> p c n", p=P)

            with sp.Fori(0, DEPTH) as l:
                for u in range(4):
                    sp.wait_ge(split_ready, l * GRANULES + 2 * u + 2)
                    load(u, block_of(w_ada, l * D + 512 * u, 0))
                with sp.Fori(1, ADA_FIRST) as i:
                    for u in range(4):
                        sp.wait_ge(ada_used, l * ADA_UNITS + i * 4 + (u - 3))
                        load(u, block_of(w_ada, l * D + 512 * u, i * 256))
                for u in range(4):
                    sp.wait_ge(ada_used, l * ADA_UNITS + (4 * ADA_FIRST - 3 + u))
                    load(u, block_of(w_in, l * D + 512 * u, 0, 192), 192)
                with sp.Fori(1, 4) as i:
                    for u in range(4):
                        unit(l, i * 4 + u, u, block_of(w_in, l * D + 512 * u, i * 192, 192), 192)
                n0 = 16
                for col, width in ((768, 256), (1024, 256), (1280, 256), (1552, 256), (1536, RANK)):
                    for u in range(4):
                        unit(l, n0 + u, u, block_of(w_in, l * D + 512 * u, col, width), width)
                    n0 += 4
                with sp.Fori(0, 16) as i:
                    for u in range(4):
                        unit(l, i * 4 + n0 + u, u, block_of(w_in, l * D + 512 * u, i * 256 + 1808))
                n0 += 64
                for u in range(2):
                    unit(l, n0 + u, u, block_of(w_out, l * D + 512 * u, 0))
                for u in range(4):
                    sp.wait_ge(split_ready, l * GRANULES + 2 * (LATE_AT + u) + 2)
                    load((2 + u) % 4, block_of(w_ada, l * D + 512 * u, 256 * ADA_FIRST))
                with sp.Fori(1, ADA_LATE // 4) as i:
                    for u in range(4):
                        sp.wait_ge(ada_used, l * ADA_UNITS + i * 4 + (4 * ADA_FIRST - 3 + u))
                        load((2 + u) % 4, block_of(w_ada, l * D + 512 * u, i * 256 + 256 * ADA_FIRST))
                for u in range(2, 6):
                    sp.wait_ge(ada_used, l * ADA_UNITS + (ADA_UNITS - 5 + u))
                    load(u % 4, block_of(w_out, l * D + 512 * (u % 4), u // 4 * 256))
                for u in range(6, 8):
                    unit(l, n0 + u, u % 4, block_of(w_out, l * D + 512 * (u % 4), 256))
                with sp.Fori(2, 8) as i:
                    for u in range(4):
                        unit(l, i * 4 + n0 + u, u, block_of(w_out, l * D + 512 * u, i * 256))
                n0 += 32
                first = 0
                for n, k in zip(PARTS, DOWN_K):
                    with sp.Fori(0, n) as i:
                        for side in range(2):
                            for u in range(4):
                                unit(l, i * 8 + n0 + 4 * side + u, u,
                                     block_of(w_up, l * D + 512 * u, i * 256 + first * 256 + side * D_FF))
                    n0 += 8 * n
                    step = 4 if k == 3 else 1
                    with sp.Fori(0, 8 // step) as i:
                        for j in range(step):
                            for u in range(k):
                                unit(l, i * (step * k) + n0 + j * k + u, (j * k + u) % 4,
                                     block_of(w_down, l * D_FF + first * 256 + 512 * u, i * (256 * step) + 256 * j))
                    n0 += 8 * k
                    first += n

        @block.gpsimd
        def _(pool):
            def hold(s, v):
                pool.wait_ge(s, v)
                pool.sem_inc(credits, 1)

            pool.dma_start(CST[:], I["k_cst"]).then_inc(consts_in, 16)
            pool.dma_start(KEEP[:], I["k_keep"]).then_inc(consts_in, 16)
            pool.dma_start(CIN[0:1, :], I["c_prompt"]).then_inc(inputs_in, 16)
            pool.dma_start(CIN[1:9, :], I["c_sample"]).then_inc(inputs_in, 16)
            for t in range(2):
                pool.dma_start(XIN[:, t, :], I["x_prompt"][0, 128 * t:128 * t + 128, :]).then_inc(inputs_in, 16)
            pool.dma_start(XIN[0:64, 2, :], I["x_sample"].rearrange("b t d -> (b t) d")).then_inc(inputs_in, 16)
            with pool.Fori(0, DEPTH) as l:
                hold(stage_free, l + 1)

                def rows(name, tile, r0, n, width=128):
                    src = I[name]
                    if len(src.shape) == 3:
                        src = src.rearrange("l a n -> l (a n)")
                    src = src[bass.ds(l, 1), :].rearrange("o (k p) -> (o k) p", p=width)
                    pool.dma_start(STG[r0:r0 + n, tile, 0:width], src).then_inc(params_in, 16)

                rows("norm1_g", 0, 0, 16)
                rows("norm2_g", 0, 16, 16)
                rows("b_ada", 0, 32, 96)
                rows("gla_norm_g", 1, 0, 6)
                rows("lru_conv_w", 1, 6, 24)
                rows("lru_conv_b", 1, 30, 6)
                rows("lru_b_a", 1, 36, 6)
                rows("lru_b_x", 1, 42, 6)
                rows("lru_lambda", 1, 48, 6)
                rows("ret_norm_g", 1, 54, 4)
                pool.dma_start(STG[58:74, 1, :], I["final_g"].rearrange("(k p) -> k p", p=128)).then_inc(params_in, 16)
                for k in range(3):
                    src = I["ffn_conv_w"][bass.ds(l, 1), k, :].rearrange("o (k p) -> (o k) p", p=128)
                    pool.dma_start(STG[0:NB_FF, 2 + k, :], src).then_inc(params_in, 16)
                rows("ffn_conv_b", 5, 0, NB_FF)
                rows("gla_b_alpha", 6, 0, 4, DK)
                src = I["gla_w_alpha"].rearrange("l r n -> (l r) n")[bass.ds(l * RANK, RANK), :]
                pool.dma_start(WAL[:], src).then_inc(params_in, 16)

                hold(hn_ready, l * 32 + 16)
                pool.dma_start(MSK[:], I["k_masks"]).then_inc(masks_in, 16)
                hold(masks_in, l * 16 + 16)
                pool.tensor_copy(GM[:], MSK[:]).then_inc(masks_ready, 1)

                def state_load(dst, src, n):
                    if n % 4:
                        hold(state_out, l * 256 + 32 * n)
                    pool.dma_start(dst, src).then_inc(state_in, 16)

                def state_store(src_s, src_p, dst_s, dst_p, n):
                    hold(state_new, l * 8 + n)
                    pool.dma_start(dst_s, src_s).then_inc(state_out, 16)
                    pool.dma_start(dst_p, src_p).then_inc(state_out, 16)

                def by_head(ap, h):
                    return ap[bass.ds(l, 1), :, h, :, :].rearrange("o b d v -> d (o b) v")

                for h in range(H):
                    state_load(ST[:, 0:NS, :], by_head(I["state_gla"], h), h)
                    state_store(ST[:, 0:NS, :], ST[:, 9:10, :], by_head(O["gla_s"], h), by_head(O["gla_p"], h), h + 1)

                hold(state_out, l * 256 + 128)
                hold(mix_ready, l * 3 + 1)
                for g in range(2):
                    pool.memset(GW[g][:], 0.0).then_inc(gw_zero, 1)
                hold(gw_zero, l * 2 + 2)
                for g, name in ((0, "lru_w_a"), (1, "lru_w_x")):
                    src = I[name].rearrange("l (q h) i j -> (l q) h i j", h=4)[bass.ds(l * 2, 2)]
                    dst = GW[g][:].rearrange("p (q k) c -> p q k c", k=3)
                    for k, p0, hh, i0, n, c0 in ((0, 0, 0, 0, 96, 0), (0, 96, 1, 0, 32, 96), (1, 0, 1, 32, 64, 0),
                                                 (1, 64, 2, 0, 64, 96), (2, 0, 2, 64, 32, 0), (2, 32, 3, 0, 96, 96)):
                        pool.dma_start(dst[p0:p0 + n, :, k, c0:c0 + 96],
                                       src[:, hh, i0:i0 + n, :].rearrange("q i j -> i q j")).then_inc(lru_in, 16)
                pool.dma_start(SLC[:], I["state_lru_conv"].rearrange("l b k w -> (l b k) w")[bass.ds(l * 24, 24), :]).then_inc(lru_in, 16)
                pool.dma_start(SLH[:], I["state_lru"].rearrange("l b w -> (l b) w")[bass.ds(l * 8, 8), :]).then_inc(lru_in, 16)
                hold(lru_rows, l * 2 + 1)
                pool.dma_start(O["lconv_p"].rearrange("l b k w -> (l b k) w")[bass.ds(l * 3, 3), :], OLC[0:3, :]).then_inc(lru_out, 16)
                pool.dma_start(O["lconv_s"].rearrange("l b k w -> (l b k) w")[bass.ds(l * 24, 24), :], OLC[3:27, :]).then_inc(lru_out, 16)
                hold(lru_rows, l * 2 + 2)
                pool.dma_start(O["lru_p"].rearrange("l b w -> (l b) w")[bass.ds(l, 1), :], OLH[0:1, :]).then_inc(lru_out, 16)
                pool.dma_start(O["lru_s"].rearrange("l b w -> (l b) w")[bass.ds(l * 8, 8), :], OLH[1:9, :]).then_inc(lru_out, 16)

                hold(mix_ready, l * 3 + 2)
                for t, name in ((COS, "k_cos"), (SIN, "k_sin"), (RD, "k_rd"), (QD, "k_qd"), (KD, "k_kd")):
                    pool.dma_start(t[:], I[name]).then_inc(rtab_in, 16)
                for h in range(H):
                    state_load(RST[:, 0:NS, :], by_head(I["state_ret"], h), 4 + h)
                    state_store(RST[:, 0:NS, :], RST[:, 9:10, :], by_head(O["ret_s"], h), by_head(O["ret_p"], h), 4 + h + 1)

                hold(state_out, l * 256 + 256)
                hold(mix_ready, l * 3 + 3)
                src = I["state_ffn_conv"].rearrange("l b k w -> (l b k) w")[bass.ds(l * 16, 16), :]
                pool.dma_start(STF[:], src).then_inc(hist_in, 16)
            for t in range(3):
                pool.wait_ge(y_rows, t + 1)
                if t < 2:
                    pool.dma_start(O["y_p"][0, 128 * t:128 * t + 128, :], YO[:, t, :]).then_inc(y_out, 16)
                else:
                    pool.dma_start(O["y_s"].rearrange("b t d -> (b t) d"), YO[0:64, 2, :]).then_inc(y_out, 16)
            pool.wait_ge(state_out, DEPTH * 256)
            pool.wait_ge(lru_out, DEPTH * 64)
            for b in range(2):
                pool.wait_ge(rows_out[b], DEPTH * 352)
            pool.wait_ge(y_out, 48)

        @block.scalar
        def _(act):
            A = nc.scalar.activation

            def drain():
                nc.scalar.drain()

            def signal(s, n=1):
                nc.scalar.drain().then_inc(s, n)

            def his(l, rounds, first, n=8):
                for g in range(first, first + n):
                    s, half, value = loaded(l, rounds, g)
                    if half == 0:
                        act.wait_ge(raw_loaded[s], value)
                    act.wait_ge(split_used, l * GRANULES + rounds * 8 + (g + 1))
                    A(WHI[:, g % 4], RAW[:, s, half:half + 2, :], ACT.Copy).then_inc(hi_ready, 1)

            late = [0]

            def late_rows(l, name):
                if JOB[name][0] != 1:
                    return
                units = min(JOB[name][1] - JOB["alpha0"][1], ADA_LATE)
                while 4 * (late[0] + 1) <= units:
                    q = late[0]
                    act.wait_ge(ada_used, l * ADA_UNITS + 4 * (ADA_FIRST + q + 1))
                    A(ROWS[:, 256 * q:256 * q + 256], PS[0:9, q % 2 * 2, 0:256], ACT.Copy).then_inc(pair_free[q % 2], 1)
                    late[0] += 1

            def take(name, l, out, cols, rows=slice(0, P), func=ACT.Copy, **kw):
                late_rows(l, name)
                act.wait_ge(job_done, job_value(name, l))
                src = bank(name)[rows, cols[0]:cols[1]]
                if len(out.shape) == 3:
                    src = src.rearrange("p (a b) -> p a b", a=out.shape[1])
                return A(out, src, func, **kw)

            def squares(k):
                A(SQ[:, 4 * k:4 * k + 4], X[:, 4 * k:4 * k + 4], ACT.Square).then_inc(sq_ready, 1)

            def squares_after(l, q, done, base):
                if q % 2 == 0:
                    act.wait_ge(done, base + q)
                    squares(q // 2 - 1)

            def root(value):
                act.wait_ge(ms_ready, value)
                A(RS[:], RS[:], ACT.Sqrt).then_inc(rms_ready, 1)

            def hn_his(l, n, sc, sh, first):
                for i in range(KC // 2):
                    act.wait_ge(hn_f32, l * 32 + 16 * n + 2 * i + 2)
                    s = i % 3 * 2
                    for j in range(2):
                        c = 2 * i + j
                        A(NT[:, s + j, SP], NT[:, s + j, SP], ACT.Identity, scale=MOD[:, sc + c, 0:1], bias=MOD[:, sh + c, 0:1])
                    drain()
                    A(HH[:, 2 * i:2 * i + 2], NT[:, s:s + 2], ACT.Copy).then_inc(hn_hi, 1)
                    if 3 <= i < 7:
                        his(l, 0, first + i - 3, 1)

            act.wait_ge(job_done, job_value("c", 0))
            A(CACT[:], bank("c")[:, 0:144].rearrange("p (k s) -> p k s", k=KC), ACT.Silu).then_inc(freed("c"), 1)
            signal(c_ready)

            act.wait_ge(x_new, 1)
            for k in range(4):
                squares(k)
            with act.Fori(0, DEPTH) as l:
                root(l * 2 + 1)
                with act.Fori(0, ADA_FIRST // 2) as i:
                    for j in range(2):
                        act.wait_ge(ada_used, l * ADA_UNITS + i * 8 + (4 * j + 4))
                        A(ROWS[:, bass.ds(i * 512 + 256 * j, 256)], PS[0:9, 2 * j, 0:256], ACT.Copy).then_inc(pair_free[j], 1)
                signal(rows_mod)
                his(l, 0, 0, LOOK)
                hn_his(l, 0, SC1, SH1, LOOK)

                for q in range(4):
                    pr = q % 2
                    if q:
                        his(l, 0, 8 * q + LOOK)
                    else:
                        his(l, 0, LOOK + 4, 4)
                    act.wait_ge(split_used, panel_used(l, 8 * q + 8))
                    A(Z[0:DK, 2 * q:2 * q + 2, :], PS[0:DK, 2 * pr:2 * pr + 2, 0:T], ACT.Copy).then_inc(pair_free[pr], 1)
                for j in range(4):
                    his(l, 0, G_V + 8 * j + LOOK)
                    act.wait_ge(split_used, panel_used(l, G_V + 8 * j + 8))
                    pr = j % 2
                    A(Z[:, 8 + 2 * j:10 + 2 * j, :], PS[:, 2 * pr:2 * pr + 2, 0:T], ACT.Copy).then_inc(pair_free[pr], 1)
                his(l, 0, G_GLR + LOOK)
                take("glr", l, TMP[0:RANK, 0, :], (0, T), slice(0, RANK)).then_inc(freed("glr"), 1)
                signal(glr_ready)
                with act.Fori(0, 8) as i:
                    for j in range(2):
                        his(l, i * 2 + j, G_REST + LOOK)
                        act.wait_ge(split_used, panel_used(l, i * 16 + G_REST + 8 * j + 8))
                        A(Z[:, bass.ds(i * 4 + (16 + 2 * j), 2), :], PS[:, 2 * j:2 * j + 2, 0:T], ACT.Copy).then_inc(pair_free[j], 1)
                drain()
                A(Z[0:DK, 0:4, :], Z[0:DK, 0:4, :], ACT.Copy, scale=QSCALE)
                signal(z_ready)

                act.wait_ge(alpha_in, l + 1)
                A(LA2[:], DE[:], ACT.Abs)
                drain()
                A(LA2[:], LA2[:], ACT.Exp, scale=-1.0)
                drain()
                A(LA2[:], LA2[:], ACT.Ln, bias=1.0).then_inc(softp, 1)
                act.wait_ge(masks_ready, l + 1)
                for t, (_, n) in enumerate(tiles):
                    take(f"vt{t}_0", l, VTM[0:n, t, 0:512], (0, 512), slice(0, n)).then_inc(freed(f"vt{t}_0"), 1)
                    take(f"vt{t}_1", l, VTM[0:n, t, 512:768], (0, 256), slice(0, n)).then_inc(freed(f"vt{t}_1"), 1)
                signal(v_ready)
                for h in range(H):
                    for k in range(7):
                        n = T if LEVELS[k] <= 4 else SEQ
                        act.wait_ge(diff_ready, l * 32 + (8 * h + k + 1))
                        A(DE[:, k % 2, 0:n], DE[:, k % 2, 0:n], ACT.Abs)
                        drain()
                        A(DE[:, k % 2, 0:n], DE[:, k % 2, 0:n], ACT.Exp, scale=-1.0).then_inc(decay_ready, 1)
                        if k:
                            late_rows(l, f"lev{h}_{k - 1}")
                    act.wait_ge(diff_ready, l * 32 + (8 * h + 8))
                    A(DE[:, 2, :], DE[:, 2, :], ACT.Exp)
                    A(DE[:, 3, :], BC[:, h, :], ACT.Exp)
                    A(EB[:, h % 2, 0:2], BC[:, h, 127:256:128], ACT.Exp)
                    A(EB[:, h % 2, 2:10], BC[:, h, 263:320:8], ACT.Exp)
                    signal(decay_ready)
                    take(f"kt{h}", l, KTM[:, 0:2, :], (0, 192))
                    take(f"kt{h}", l, KTM[0:64, 2, :], (192, 288), slice(0, 64)).then_inc(freed(f"kt{h}"), 1)
                    signal(ktm_ready)
                    take(f"kv{h}_0", l, ST[:, 8, :], (0, DV), slice(0, DK)).then_inc(freed(f"kv{h}_0"), 1)
                    signal(s1_ready)
                    for i, (tile, r0, n, _) in enumerate(gla_segments(h)):
                        take(f"o{h}_{i}", l, Z[r0:r0 + n, 8 + tile, :], (0, T), slice(r0, r0 + n)).then_inc(freed(f"o{h}_{i}"), 1)
                drain()
                A(Z[:, 0:6, :], Z[:, 8:14, :], ACT.Square).then_inc(osq_ready, 1)
                A(Z[:, 14:20, :], Z[:, 14:20, :], ACT.Silu).then_inc(gates_ready, 1)
                late_rows(l, "hs")
                act.wait_ge(hms_ready, l * 2 + 1)
                A(TMP[0:H, 1, :], TMP[0:H, 1, :], ACT.Sqrt).then_inc(hrms_ready, 1)
                late_rows(l, "bc5")
                act.wait_ge(mix_f32, l * 3 + 1)
                A(MH[:, 0:6, :], Z[:, 8:14, :], ACT.Copy).then_inc(mix_hi, 1)

                drain()
                A(XE[:, :, 3:259], Z[:, 20:26, SP], ACT.Copy)
                A(XE[:, :, 259:347].rearrange("p j (b k) -> p j b k", k=11)[:, :, :, 3:11],
                  Z[:, 20:26, SS].rearrange("p j (b k) -> p j b k", k=TS), ACT.Copy)
                signal(xe_ready)
                A(C8[:, 0, :], PAR[:, C_LAM:C_LAM + 6], ACT.Abs)
                drain()
                A(C8[:, 0, :], C8[:, 0, :], ACT.Exp, scale=-1.0)
                drain()
                A(C8[:, 0, :], C8[:, 0, :], ACT.Ln, bias=1.0).then_inc(softp, 1)
                take("lco0", l, OLC[:, 0:512], (0, 512), slice(0, 27)).then_inc(freed("lco0"), 1)
                take("lco1", l, OLC[:, 512:768], (0, 256), slice(0, 27)).then_inc(freed("lco1"), 1)
                signal(lru_rows)
                for j in range(6):
                    for g, (dst, c) in enumerate(((GR, C_BA), (GI, C_BX))):
                        take(f"gate{g}_{j}", l, dst[:, j, :], (0, T), func=ACT.Sigmoid,
                             bias=PAR[:, c + j:c + j + 1]).then_inc(freed(f"gate{g}_{j}"), 1)
                signal(ri_ready)
                A(Z[:, 26:32, :], Z[:, 26:32, :], ACT.Gelu_apprx_tanh).then_inc(gates_ready, 1)
                act.wait_ge(la_ready, l + 1)
                A(AA[:], GR[:], ACT.Exp)
                drain()
                A(GR[:], GR[:], ACT.Tanh, scale=-0.5).then_inc(a_ready, 1)
                act.wait_ge(em_ready, l + 1)
                A(GR[:], GR[:], ACT.Sqrt).then_inc(root_ready, 1)
                take("lho0", l, OLH[:, 0:512], (0, 512), slice(0, 9)).then_inc(freed("lho0"), 1)
                take("lho1", l, OLH[:, 512:768], (0, 256), slice(0, 9)).then_inc(freed("lho1"), 1)
                signal(lru_rows)
                act.wait_ge(lru_out, l * 64 + 64)
                act.wait_ge(mix_f32, l * 3 + 2)
                A(MH[:, 6:12, :], GR[:], ACT.Copy).then_inc(mix_hi, 1)

                act.wait_ge(mix_ready, l * 3 + 2)
                for i in range(2):
                    if i:
                        act.wait_ge(rope_done, l * 2 + 1)
                    A(ROT[0:64], Z[64:128, 32 + 4 * i:36 + 4 * i, :], ACT.Copy)
                    A(ROT[64:128], Z[0:64, 32 + 4 * i:36 + 4 * i, :], ACT.Copy)
                    signal(rot_ready)
                for t, (_, n) in enumerate(tiles):
                    take(f"rvt{t}", l, RVT[0:n, t, :], (0, 512), slice(0, n)).then_inc(freed(f"rvt{t}"), 1)
                signal(v_ready)
                act.wait_ge(rtab_in, l * 80 + 80)
                for h in range(H):
                    take(f"rkt{h}", l, RKT[:, 0:2, :], (0, 256), scale=KD[:, 0, h:h + 1])
                    take(f"rkt{h}", l, RKT[0:64, 2, :], (256, 384), slice(0, 64),
                         scale=KD[0:64, 1, h:h + 1]).then_inc(freed(f"rkt{h}"), 1)
                    signal(ktm_ready)
                    take(f"rkv{h}_0", l, RST[:, 8, :], (0, DR)).then_inc(freed(f"rkv{h}_0"), 1)
                    signal(s1_ready)
                    take(f"ro{h}", l, Z[:, 40 + h, :], (0, T)).then_inc(freed(f"ro{h}"), 1)
                drain()
                A(Z[:, 36:40, :], Z[:, 40:44, :], ACT.Square).then_inc(osq_ready, 1)
                A(Z[:, 44:48, :], Z[:, 44:48, :], ACT.Silu).then_inc(gates_ready, 1)
                late_rows(l, "rhs")
                act.wait_ge(hms_ready, l * 2 + 2)
                A(TMP[0:H, 1, :], TMP[0:H, 1, :], ACT.Sqrt).then_inc(hrms_ready, 1)
                late_rows(l, "rbc3")
                act.wait_ge(mix_f32, l * 3 + 3)
                A(MH[:, 12:16, :], Z[:, 40:44, :], ACT.Copy).then_inc(mix_hi, 1)
                signal(rows_mod)

                for q in range(8):
                    his(l, 0, G_OUT + 8 * q + LOOK)
                    if q == 2:
                        act.wait_ge(job_done, job_value("mod2", l))
                    if q:
                        squares_after(l, q, x_mid, l * 8)

                squares_after(l, 8, x_mid, l * 8)
                root(l * 2 + 2)
                hn_his(l, 1, SC2, SH2, G_UP[0] + LOOK)
                first = 0
                for p, (n, k) in enumerate(zip(PARTS, DOWN_K)):
                    with act.Fori(0, n) as i:
                        for side in range(2):
                            his(l, i * 2 + side, G_UP[p] + LOOK + (0 if side else 4), 8 if side else 4)
                            if side:
                                act.wait_ge(conv_done, l * 44 + i * 2 + (2 * first + 3))
                                A(YC[:, 0:2, 0:336], YC[:, 0:2, 0:336], ACT.Silu).then_inc(silu_done, 1)
                            act.wait_ge(split_used, panel_used(l, i * 16 + (G_UP[p] + 8 * side + 8)))
                            act.wait_ge(conv_done, l * 44 + i * 2 + (2 * first + side + 1))
                            A(EXT[:, 2 * side:2 * side + 2, 2:258], PS[:, 2 * side:2 * side + 2, SP], ACT.Copy)
                            A(EXT[:, 2 * side:2 * side + 2, 258:338].rearrange("p j (b k) -> p j b k", k=10)[:, :, :, 2:10],
                              PS[:, 2 * side:2 * side + 2, SS].rearrange("p j (b k) -> p j b k", k=TS), ACT.Copy).then_inc(pair_free[side], 1)
                            signal(ext_ready)
                        his(l, i * 2 + 2, G_UP[p] + LOOK, 4)
                        act.wait_ge(hid_f32, l * 22 + i + (first + 1))
                        A(MH[:, bass.ds(i * 2, 2), :], HF[:], ACT.Copy).then_inc(hid_hi, 1)
                    if k == 4:
                        with act.Fori(0, 8) as i:
                            his(l, i, G_DOWN[p] + LOOK + 4)
                    else:
                        job = 0
                        for q in range(8):
                            at_q, n_q = last_granules(q)
                            his(l, 0, at_q, n_q)
                            if q:
                                squares_after(l, q, x_new, l * 24 + 17)
                            for _ in range(3 if q < 6 else 2):
                                if job >= 2:
                                    act.wait_ge(rows_out[job % 2], l * 352 + 32 * (job // 2))
                                take(f"xo{job}", l, OUTF[:, job % 2, :], (0, 512), slice(0, 18)).then_inc(freed(f"xo{job}"), 1)
                                drain()
                                act.dma_start(O["fconv_p"].rearrange("l b k w -> (l b k) w")[bass.ds(l * 2, 2), 512 * job:512 * job + 512],
                                              OUTF[0:2, job % 2, :]).then_inc(rows_out[job % 2], 16)
                                act.dma_start(O["fconv_s"].rearrange("l b k w -> (l b k) w")[bass.ds(l * 16, 16), 512 * job:512 * job + 512],
                                              OUTF[2:18, job % 2, :]).then_inc(rows_out[job % 2], 16)
                                job += 1
                    first += n
                squares_after(l, 8, x_new, l * 24 + 17)
                for b in range(2):
                    act.wait_ge(rows_out[b], l * 352 + 352)

            root(DEPTH * 2 + 1)
            for t, (_, n) in enumerate(tiles):
                for k in range(4):
                    take(f"y{t}_{k}", 0, YO[0:n, t, 512 * k:512 * k + 512], (0, 512), slice(0, n)).then_inc(freed(f"y{t}_{k}"), 1)
                signal(y_rows)

        @block.vector
        def _(dve):
            V = nc.vector
            HHf, MHf = HH[:].bitcast(f32), MH[:].bitcast(f32)

            def drain():
                V.drain()

            def signal(s, n=1):
                V.drain().then_inc(s, n)

            def los(l, rounds, first, n=8):
                for g in range(first, first + n):
                    s, half, _ = loaded(l, rounds, g)
                    dve.wait_ge(hi_ready, l * GRANULES + rounds * 8 + (g + 1))
                    V.tensor_tensor(WLO[:, g % 4], RAW[:, s, half:half + 2, :], WHI[:, g % 4].bitcast(f32),
                                    ALU.subtract).then_inc(split_ready, 1)

            def job_wait(name, l):
                dve.wait_ge(job_done, job_value(name, l))

            def rms(l, n, name, count):
                job_wait(name, l)
                V.tensor_scalar(RS[:], bank(name)[:, 0:T], 1.0 / D, EPS, ALU.mult, ALU.add).then_inc(freed(name), 1)
                signal(ms_ready)
                dve.wait_ge(rms_ready, l * 2 + n + 1)
                V.reciprocal(RS[:], RS[:])
                drain()

            def apply_norm(l, n, sc, sh, first):
                def low(i):
                    dve.wait_ge(hn_hi, l * 16 + 8 * n + i + 1)
                    V.tensor_tensor(HL[:, 2 * i:2 * i + 2], NT[:, i % 3 * 2:i % 3 * 2 + 2], HHf[:, 2 * i:2 * i + 2],
                                    ALU.subtract).then_inc(hn_ready, 2)
                    if 2 <= i < 6:
                        los(l, 0, first + i - 2, 1)

                for i in range(KC // 2):
                    c, nt = 2 * i, NT[:, i % 3 * 2:i % 3 * 2 + 2]
                    V.tensor_tensor(nt, X[:, c:c + 2], RS[:].unsqueeze(1).broadcast_to([P, 2, T]), ALU.mult)
                    drain()
                    nt = nt[:, :, SS].rearrange("p j (b k) -> p j b k", k=TS)
                    V.tensor_tensor(nt, nt, MOD[:, sc + c:sc + c + 2, 1:9].unsqueeze(3).broadcast_to([P, 2, NS, TS]), ALU.mult)
                    drain()
                    V.tensor_tensor(nt, nt, MOD[:, sh + c:sh + c + 2, 1:9].unsqueeze(3).broadcast_to([P, 2, NS, TS]), ALU.add)
                    signal(hn_f32, 2)
                    if i:
                        low(i - 1)
                low(KC // 2 - 1)
                drain()

            def modulation(l, name, first):
                job_wait(name, l)
                V.tensor_tensor(MOD[:, first:first + 32, :], bank(name)[:, 0:288].rearrange("p (m s) -> p m s", s=9),
                                PAR[:, C_BADA + first:C_BADA + first + 32].unsqueeze(2).broadcast_to([P, 32, 9]),
                                ALU.add).then_inc(freed(name), 1)
                drain()

            def scale_by(sc, c):
                V.scalar_tensor_tensor(MOD[:, sc:sc + 16, :], MOD[:, sc:sc + 16, :], 1.0,
                                       PAR[:, c:c + 16].unsqueeze(2).broadcast_to([P, 16, 9]), ALU.add, ALU.mult)

            def add_back(l, gate, i, pr, done, value):
                drain()
                V.tensor_copy(GS[:], MOD[:, bass.ds(i * 2 + gate, 2), :])
                drain()
                dve.wait_ge(split_used, value)
                for j in range(2):
                    x = X[:, bass.ds(i * 2 + j, 1), SP]
                    V.scalar_tensor_tensor(x, PS[:, 2 * pr + j:2 * pr + j + 1, SP], GS[:, j, 0:1], x, ALU.mult, ALU.add)
                tmp = TMP[:, :, 0:64].rearrange("p j (b k) -> p j b k", k=TS)
                V.tensor_tensor(tmp, PS[:, 2 * pr:2 * pr + 2, SS].rearrange("p j (b k) -> p j b k", k=TS),
                                GS[:, :, 1:9].unsqueeze(3).broadcast_to([P, 2, NS, TS]), ALU.mult)
                V.drain().then_inc(pair_free[pr], 1)
                x = X[:, bass.ds(i * 2, 2), SS]
                V.tensor_tensor(x, x, TMP[:, :, 0:64], ALU.add)
                signal(done)

            for s, n in ((split_ready, 8), (split_used, LOOK), (pair_free[0], 1), (pair_free[1], 1), (conv_done, 2),
                         (bank_free[0], 1), (bank_free[1], 1), (bank_free[2], 1), (bank_free[3], 1)):
                dve.sem_inc(s, n)
            for t, (tok, n) in enumerate(tiles):
                for k in range(4):
                    job_wait(f"x{t}_{k}", 0)
                    V.tensor_copy(X[:, 4 * k:4 * k + 4, tok],
                                  bank(f"x{t}_{k}").rearrange("p (j t) -> p j t", j=4)[:, :, 0:n]).then_inc(freed(f"x{t}_{k}"), 1)
            signal(x_new)
            V.drain().then_inc(stage_free, 1)
            dve.wait_ge(consts_in, 32)

            with dve.Fori(0, DEPTH) as l:
                drain()
                for i, (c, n, np_) in enumerate(((0, 128, P), (128, 74, P), (256, 88, P), (344, 88, P), (432, 88, P),
                                                (520, 88, P), (C_AL, 4, DK))):
                    job_wait(f"par{i}", l)
                    V.tensor_copy(PAR[0:np_, c:c + n], bank(f"par{i}")[0:np_, 0:n]).then_inc(freed(f"par{i}"), 1)
                signal(par_ready)
                rms(l, 0, "ss1", 0)
                modulation(l, "mod0", 0)
                scale_by(SC1, C_N1)
                los(l, 0, 0, LOOK)
                drain()
                apply_norm(l, 0, SC1, SH1, LOOK)

                los(l, 0, LOOK + 4, 28)
                for j in range(4):
                    los(l, 0, G_V + 8 * j + LOOK)
                los(l, 0, G_GLR + LOOK)
                with dve.Fori(0, 16) as i:
                    los(l, i, G_REST + LOOK)

                for h in range(H):
                    job_wait(f"alpha{h}", l)
                    V.tensor_scalar(DE[:, h, :], bank(f"alpha{h}")[0:DK, 0:T], PAR[0:DK, C_AL + h:C_AL + h + 1], None,
                                    ALU.add).then_inc(freed(f"alpha{h}"), 1)
                signal(alpha_in)
                dve.wait_ge(softp, l * 2 + 1)
                V.scalar_tensor_tensor(DE[:], DE[:], 0.0, LA2[:], ALU.min, ALU.subtract)
                drain()
                V.tensor_scalar(DE[:], DE[:], 1.0 / 16.0, None, ALU.mult)
                drain()
                for h in range(H):
                    V.tensor_tensor_scan(BC[:, h, :], KEEP[0:DK, :], DE[:, h, :], 0.0, ALU.mult, ALU.add)
                drain()
                dve.wait_ge(z_ready, l + 1)
                dve.wait_ge(masks_ready, l + 1)

                for h in range(H):
                    s = h % 2
                    V.memset(ATT[:, s, :], 0.0)

                    def diff(k):
                        hs, n = LEVELS[k], T if LEVELS[k] <= 4 else SEQ
                        b = BC[:, h, 0:n].rearrange("p (n m) -> p n m", m=2 * hs)
                        V.tensor_tensor(DE[:, k % 2, 0:n].rearrange("p (n m) -> p n m", m=2 * hs), b,
                                        b[:, :, hs - 1:hs].broadcast_to([DK, n // (2 * hs), 2 * hs]),
                                        ALU.subtract).then_inc(diff_ready, 1)

                    def pick(k):
                        n = 320 if LEVELS[k] <= 4 else SEQ
                        job_wait(f"lev{h}_{k}", l)
                        dve.sem_inc(picks, 1)
                        b = bank(f"lev{h}_{k}")
                        op = V.copy_predicated(ATT[:, s, SP].rearrange("p (a t) -> p a t", a=2),
                                               GM[:, k:k + 1, 0:128].broadcast_to([P, 2, 128]),
                                               b[:, SP].rearrange("p (a t) -> p a t", a=2))
                        if n > SEQ:
                            op = V.copy_predicated(ATT[0:64, s, SS], GM[0:64, k, 128:192], b[0:64, SS])
                        op.then_inc(freed(f"lev{h}_{k}"), 1)

                    diff(0)
                    for k in range(7):
                        n = T if LEVELS[k] <= 4 else SEQ
                        drain()
                        if k < 6:
                            diff(k + 1)
                        if k:
                            pick(k - 1)
                        dve.wait_ge(decay_ready, l * 32 + (8 * h + k + 1))
                        V.tensor_tensor(QP[:, k % 2, 0:n], Z[0:DK, h, 0:n], DE[:, k % 2, 0:n], ALU.mult).then_inc(qk_ready, 1)
                        V.tensor_tensor(KP[:, k % 2, 0:n], Z[0:DK, 4 + h, 0:n], DE[:, k % 2, 0:n], ALU.mult).then_inc(qk_ready, 1)
                    for view, m in ((SP, 128), (SS, TS)):
                        b = BC[:, h, view].rearrange("p (n m) -> p n m", m=m)
                        V.tensor_tensor(DE[:, 2, view].rearrange("p (n m) -> p n m", m=m),
                                        b[:, :, m - 1:m].broadcast_to([DK, b.shape[1], m]), b, ALU.subtract)
                    signal(diff_ready)
                    pick(6)
                    drain()
                    pick(7)
                    signal(att_ready)
                    dve.wait_ge(decay_ready, l * 32 + (8 * h + 8))
                    V.tensor_tensor(KP[:, 1, :], Z[0:DK, 4 + h, :], DE[:, 2, :], ALU.mult).then_inc(qk_ready, 1)
                    V.tensor_tensor(QP[:, 1, :], Z[0:DK, h, :], DE[:, 3, :], ALU.mult).then_inc(qk_ready, 1)
                    dve.wait_ge(ktm_ready, l * 8 + (h + 1))
                    V.tensor_tensor(KTMM[:], KTM[0:64, 2:3, :].broadcast_to([64, NS, DK]),
                                    SEL.unsqueeze(2).broadcast_to([64, NS, DK]), ALU.mult).then_inc(ktmm_ready, 1)
                    dve.wait_ge(state_in, l * 128 + 16 * (h + 1))
                    job_wait(f"kv{h}_1", l)
                    V.scalar_tensor_tensor(ST[:, 9, :], ST[:, 8, :], EB[:, s, 1:2], bank(f"kv{h}_1")[0:DK, 0:DV],
                                           ALU.mult, ALU.add).then_inc(freed(f"kv{h}_1"), 1)
                    for i in range(4):
                        job_wait(f"kvs{h}_{i}", l)
                        for j in range(2):
                            b = 2 * i + j
                            op = V.scalar_tensor_tensor(ST[:, b, :], ST[:, b, :], EB[:, s, 2 + b:3 + b],
                                                        bank(f"kvs{h}_{i}")[0:DK, DV * j:DV * j + DV], ALU.mult, ALU.add)
                        op.then_inc(freed(f"kvs{h}_{i}"), 1)
                    signal(state_new)

                def head_norm(n, name, bcs, width, c, z0, gate, count):
                    job_wait(name, l)
                    V.tensor_scalar(TMP[0:H, 1, :], bank(name)[0:H, 0:T], 1.0 / width, EPS, ALU.mult, ALU.add).then_inc(freed(name), 1)
                    signal(hms_ready)
                    dve.wait_ge(hrms_ready, l * 2 + (n + 1))
                    V.reciprocal(TMP[0:H, 0, :], TMP[0:H, 1, :]).then_inc(hrs_ready, 1)
                    for j in range(count):
                        job_wait(f"{bcs}{j}", l)
                        V.scalar_tensor_tensor(Z[:, z0 + j, :], bank(f"{bcs}{j}")[:, 0:T], PAR[:, c + j:c + j + 1],
                                               Z[:, z0 + j, :], ALU.mult, ALU.mult).then_inc(freed(f"{bcs}{j}"), 1)
                    drain()
                    V.tensor_tensor(Z[:, z0:z0 + count, :], Z[:, z0:z0 + count, :], Z[:, gate:gate + count, :], ALU.mult).then_inc(mix_f32, 1)

                dve.wait_ge(gates_ready, l * 3 + 1)
                head_norm(0, "hs", "bc", DV, C_GN, 8, 14, 6)
                dve.wait_ge(mix_hi, l * 3 + 1)
                dve.wait_ge(state_out, l * 256 + 128)
                V.tensor_tensor(ML[:, 0:6, :], Z[:, 8:14, :], MHf[:, 0:6, :], ALU.subtract).then_inc(mix_ready, 1)

                V.memset(XE[:, :, 0:3], 0.0)
                job_wait("lcv", l)
                V.tensor_copy(XE[:, :, 259:347].rearrange("p j (b k) -> p j b k", k=11)[:, :, :, 0:3],
                              bank("lcv")[:, 0:144].rearrange("p (j b k) -> p j b k", j=6, k=3))
                V.tensor_copy(H0[:], bank("lcv")[:, 144:192].rearrange("p (j b) -> p j b", j=6)).then_inc(freed("lcv"), 1)
                drain()
                dve.wait_ge(xe_ready, l + 1)
                xs = XE[:, :, 259:347].rearrange("p j (b k) -> p j b k", k=11)
                V.tensor_copy(LCO[:, :, 0:3], XE[:, :, 256:259])
                V.tensor_copy(LCO[:, :, 3:27].rearrange("p j (b k) -> p j b k", k=3), xs[:, :, :, 8:11])
                signal(lco_ready)
                y = TMP[:].rearrange("p j t -> p (j t)")
                for j in range(6):
                    w = [PAR[:, C_CW + 6 * k + j:C_CW + 6 * k + j + 1] for k in range(4)]
                    V.tensor_scalar(y[:, 0:344], XE[:, j, 0:344], w[0], PAR[:, C_CB + j:C_CB + j + 1], ALU.mult, ALU.add)
                    drain()
                    for k in (1, 2):
                        V.scalar_tensor_tensor(y[:, 0:344], XE[:, j, k:k + 344], w[k], y[:, 0:344], ALU.mult, ALU.add)
                        drain()
                    V.scalar_tensor_tensor(XC[:, j, SP], XE[:, j, 3:259], w[3], y[:, SP], ALU.mult, ALU.add)
                    V.scalar_tensor_tensor(XC[:, j, SS].rearrange("p (b k) -> p b k", k=TS), xs[:, j, :, 3:11], w[3],
                                           y[:, 259:347].rearrange("p (b k) -> p b k", k=11)[:, :, 0:TS], ALU.mult, ALU.add)
                    drain()
                signal(xc_ready)
                V.tensor_scalar(C8[:, 1, :], PAR[:, C_LAM:C_LAM + 6], -1.0, 0.0, ALU.mult, ALU.max)
                drain()
                dve.wait_ge(softp, l * 2 + 2)
                V.tensor_tensor(C8[:, 2, :], C8[:, 0, :], C8[:, 1, :], ALU.add)
                drain()
                V.tensor_scalar(C8[:, 2, :], C8[:, 2, :], -8.0, None, ALU.mult)
                drain()
                dve.wait_ge(ri_ready, l + 1)
                V.tensor_tensor(GR[:], GR[:], C8[:, 2, :].unsqueeze(2).broadcast_to([P, 6, T]), ALU.mult).then_inc(la_ready, 1)
                V.tensor_tensor(GI[:], GI[:], XC[:], ALU.mult)
                drain()
                dve.wait_ge(a_ready, l + 1)
                V.scalar_tensor_tensor(GR[:], AA[:], 1.0, GR[:], ALU.add, ALU.mult)
                drain()
                V.scalar_tensor_tensor(GR[:], AA[:], 1.0, GR[:], ALU.add, ALU.mult).then_inc(em_ready, 1)
                a0, u0 = AA[:, :, 256:320:8], GI[:, :, 256:320:8]
                V.tensor_tensor(U0[:], a0, H0[:], ALU.mult)
                drain()
                V.memset(a0, 0.0)
                dve.wait_ge(root_ready, l + 1)
                V.tensor_tensor(GI[:], GI[:], GR[:], ALU.mult)
                drain()
                V.tensor_tensor(u0, u0, U0[:], ALU.add)
                drain()
                for j in range(6):
                    V.tensor_tensor_scan(XC[:, j, :], AA[:, j, :], GI[:, j, :], 0.0, ALU.mult, ALU.add)
                drain()
                V.tensor_copy(LHO[:, :, 0:1], XC[:, :, 255:256])
                V.tensor_copy(LHO[:, :, 1:9], XC[:, :, 263:320:8])
                signal(lho_ready)
                dve.wait_ge(gates_ready, l * 3 + 2)
                V.tensor_tensor(GR[:], XC[:], Z[:, 26:32, :], ALU.mult).then_inc(mix_f32, 1)
                dve.wait_ge(mix_hi, l * 3 + 2)
                V.tensor_tensor(ML[:, 6:12, :], GR[:], MHf[:, 6:12, :], ALU.subtract).then_inc(mix_ready, 1)

                dve.wait_ge(rtab_in, l * 80 + 80)
                for i in range(2):
                    z = Z[:, 32 + 4 * i:36 + 4 * i, :]
                    dve.wait_ge(rot_ready, l * 2 + (i + 1))
                    V.tensor_tensor(z, z, COS[:].unsqueeze(1).broadcast_to([P, H, T]), ALU.mult)
                    V.tensor_tensor(ROT[:], ROT[:], SIN[:].unsqueeze(1).broadcast_to([P, H, T]), ALU.mult)
                    drain()
                    V.tensor_tensor(z, z, ROT[:], ALU.add)
                    signal(rope_done)
                for h in range(H):
                    s = h % 2
                    V.tensor_tensor(RQE[:, s, :], Z[:, 32 + h, :], QD[:, h, :], ALU.mult)
                    job_wait(f"rqk{h}", l)
                    b = bank(f"rqk{h}")
                    V.tensor_tensor(RAT[:, s, SP].rearrange("p (a t) -> p a t", a=2), b[:, SP].rearrange("p (a t) -> p a t", a=2),
                                    RD[:, h:h + 1, 0:128].broadcast_to([P, 2, 128]), ALU.mult)
                    V.tensor_tensor(RAT[0:64, s, SS], b[0:64, SS], RD[0:64, h, 128:192], ALU.mult).then_inc(freed(f"rqk{h}"), 1)
                    signal(att_ready)
                    dve.wait_ge(ktm_ready, l * 8 + (h + 5))
                    V.tensor_tensor(RKM[:], RKT[0:64, 2:3, :].broadcast_to([64, NS, DR]),
                                    SEL.unsqueeze(2).broadcast_to([64, NS, DR]), ALU.mult).then_inc(ktmm_ready, 1)
                    dve.wait_ge(state_in, l * 128 + 16 * (h + 5))
                    g = math.exp(128 * math.log1p(-2.0 ** (-5 - h))), math.exp(TS * math.log1p(-2.0 ** (-5 - h)))
                    job_wait(f"rkv{h}_1", l)
                    V.scalar_tensor_tensor(RST[:, 9, :], RST[:, 8, :], g[0], bank(f"rkv{h}_1")[:, 0:DR],
                                           ALU.mult, ALU.add).then_inc(freed(f"rkv{h}_1"), 1)
                    for i in range(2):
                        job_wait(f"rkvs{h}_{i}", l)
                        st = RST[:, 4 * i:4 * i + 4, :]
                        V.scalar_tensor_tensor(st, st, g[1], bank(f"rkvs{h}_{i}").rearrange("p (a b) -> p a b", a=4),
                                               ALU.mult, ALU.add).then_inc(freed(f"rkvs{h}_{i}"), 1)
                    signal(state_new)
                dve.wait_ge(gates_ready, l * 3 + 3)
                head_norm(1, "rhs", "rbc", DR, C_RN, 40, 44, 4)
                dve.wait_ge(mix_hi, l * 3 + 3)
                V.tensor_tensor(ML[:, 12:16, :], Z[:, 40:44, :], MHf[:, 12:16, :], ALU.subtract).then_inc(mix_ready, 1)

                modulation(l, "mod1", 32)
                modulation(l, "mod2", 64)
                scale_by(SC2, C_N2)
                job = 0
                for q in range(8):
                    los(l, 0, G_OUT + 8 * q + LOOK)
                    for _ in range(3 if q < 6 else 2):
                        job_wait(f"hist{job}", l)
                        V.tensor_copy(HIST[:, 4 * job:4 * job + 4, :],
                                      bank(f"hist{job}")[:, 0:64].rearrange("p (a b) -> p a b", a=4)).then_inc(freed(f"hist{job}"), 1)
                        job += 1
                    add_back(l, GA1, q, q % 2, x_mid, panel_used(l, G_OUT + 8 * q + 8))

                signal(stage_free)
                rms(l, 1, "ss2", 1)
                apply_norm(l, 1, SC2, SH2, G_UP[0] + LOOK)

                V.memset(EXT[:, :, 0:2], 0.0)
                drain()
                first = 0
                for p, (n, k) in enumerate(zip(PARTS, DOWN_K)):
                    with dve.Fori(0, n) as i:
                        for side in range(2):
                            e = EXT[:, 2 * side:2 * side + 2]
                            es = e[:, :, 258:338].rearrange("p j (b k) -> p j b k", k=10)
                            blk = i * 2 + (44 * side + 2 * first)
                            los(l, i * 2 + side, G_UP[p] + LOOK + (0 if side else 4), 8 if side else 4)
                            V.tensor_copy(CW[:, side], PAR[:, C_FF:608].rearrange("p (k j) -> p k j", k=4)[:, :, bass.ds(blk, 2)])
                            V.tensor_copy(es[:, :, :, 0:2], HIST[:, bass.ds(blk, 2), :].rearrange("p j (b k) -> p j b k", k=2))
                            drain()
                            dve.wait_ge(ext_ready, l * 44 + i * 2 + (2 * first + side + 1))
                            V.tensor_copy(XO[:, bass.ds(blk, 2), 0:2], e[:, :, 256:258])
                            V.tensor_copy(XO[:, bass.ds(blk, 2), 2:18].rearrange("p j (b k) -> p j b k", k=2), es[:, :, :, 8:10])
                            for j in range(2):
                                V.tensor_scalar(YC[:, 2 * side + j, 0:336], e[:, j, 0:336], CW[:, side, 0, j:j + 1],
                                                CW[:, side, 3, j:j + 1], ALU.mult, ALU.add)
                            for tap in (1, 2):
                                drain()
                                for j in range(2):
                                    y = YC[:, 2 * side + j, 0:336]
                                    V.scalar_tensor_tensor(y, e[:, j, tap:tap + 336], CW[:, side, tap, j:j + 1], y, ALU.mult, ALU.add)
                            signal(conv_done)
                        los(l, i * 2 + 2, G_UP[p] + LOOK, 4)
                        dve.wait_ge(silu_done, l * 22 + i + (first + 1))
                        ys = YC[:, :, 258:338].rearrange("p j (b k) -> p j b k", k=10)[:, :, :, 0:TS]
                        V.tensor_tensor(HF[:, :, SP], YC[:, 0:2, SP], YC[:, 2:4, SP], ALU.mult)
                        V.tensor_tensor(HF[:, :, SS].rearrange("p j (b k) -> p j b k", k=TS), ys[:, 0:2], ys[:, 2:4], ALU.mult)
                        signal(hid_f32)
                        dve.wait_ge(hid_hi, l * 22 + i + (first + 1))
                        V.tensor_tensor(ML[:, bass.ds(i * 2, 2), :], HF[:], MHf[:, bass.ds(i * 2, 2), :], ALU.subtract).then_inc(hid_ready, 1)
                    if k == 4:
                        with dve.Fori(0, 4) as i:
                            for j in range(2):
                                los(l, i * 2 + j, G_DOWN[p] + LOOK + 4)
                                add_back(l, GA2, i * 2 + j, j, x_new, panel_used(l, i * 16 + (G_DOWN[p] + 8 * j + 8)))
                    else:
                        for q in range(8):
                            at_q, n_q = last_granules(q)
                            los(l, 0, at_q, n_q)
                            add_back(l, GA2, q, q % 2, x_new, panel_used(l, G_DOWN[p] + 6 * q + 6))
                    first += n

            job_wait("ssf", 0)
            V.tensor_scalar(RS[:], bank("ssf")[:, 0:T], 1.0 / D, EPS, ALU.mult, ALU.add).then_inc(freed("ssf"), 1)
            signal(ms_ready)
            dve.wait_ge(rms_ready, DEPTH * 2 + 1)
            V.reciprocal(RS[:], RS[:])
            drain()
            for k in range(KC):
                V.scalar_tensor_tensor(SQ[:, k, :], X[:, k, :], PAR[:, C_FG + k:C_FG + k + 1], RS[:], ALU.mult, ALU.mult).then_inc(hn_f32, 1)

        @block.tensor
        def _(pe):
            def mm(out, w, x, start, stop):
                return nc.tensor.matmul(out, w, x, start=start, stop=stop)

            def more(out, w, x):
                return nc.tensor.matmul(out, w, x, start=False, stop=True, skip_group_check=True)

            def begin(name, l):
                pe.wait_ge(freed(name), bank_value(name, l))
                return bank(name)

            def granules(l, rounds, first, k0, pr, act_h, act_l, widths, last, n, ready=None, out=None):
                for g in range(n):
                    c = 2 * g
                    if ready is not None:
                        ready(k0 + c + 2)
                    pe.wait_ge(split_ready, l * GRANULES + rounds * 8 + (first + g + 9))
                    s = (first + g) % 4
                    for kk in range(2):
                        for j, (c0, w) in enumerate(widths):
                            dst = PS[0:w, 2 * pr + j, 0:T] if out is None else out[0:w, 0:T]
                            kc = k0 + c + kk
                            hi, lo = WHI[:, s, kk, c0:c0 + w], WLO[:, s, kk, c0:c0 + w]
                            mm(dst, hi, act_h[:, kc, :], kc == 0, False)
                            mm(dst, hi, act_l[:, kc, :], False, False)
                            op = mm(dst, lo, act_h[:, kc, :], False, kc == last)
                    if out is None or g < n - 1:
                        op.then_inc(split_used, 1)
                    else:
                        op.then_inc(job_done, 1)
                        nc.tensor.drain().then_inc(split_used, 1)

            FULL = ((0, 128), (128, 128))

            def panel(l, rounds, first, pr, free, act_h, act_l, widths=FULL, n=8, ready=None):
                pe.wait_ge(pair_free[pr], free)
                granules(l, rounds, first, 0, pr, act_h, act_l, widths, 2 * n - 1, n, ready)

            def ones_sum(name, l, value):
                b = begin(name, l)
                for k in range(KC):
                    if k % 4 == 0:
                        pe.wait_ge(sq_ready, value + k // 4 + 1)
                    op = mm(b[:, 0:T], ONES, SQ[:, k, :], k == 0, k == KC - 1)
                op.then_inc(job_done, 1)

            def ada_unit(u, s, value, pr):
                pe.wait_ge(raw_loaded[s], value)
                for c in range(4):
                    op = mm(PS[0:9, 2 * pr, 0:256], CACT[:, 4 * u + c, :], RAW[:, s, c, :],
                            4 * u + c == 0, 4 * u + c == KC - 1)
                op.then_inc(ada_used, 1)

            def ahead(name, l):
                if name in LATE:
                    v = LATE[name]
                    q, u = v // 4, v % 4
                    if u == 0:
                        pe.wait_ge(pair_free[q % 2], pair_value(l, (Q_LATE + q) // 2))
                    pos = 4 * ADA_FIRST + LATE_AT + v
                    ada_unit(u, pos % 4, (l * (UNITS // 4) + (pos // 4 + 1)) * 16, q % 2)

            def mod_turn(l, k):
                pe.wait_ge(rows_mod, l * 2 + k + 1)
                for i in range(k + 1):
                    turn(f"mod{k + i}", l, [(bank(f"mod{k + i}")[:, 9 * m:9 * m + 9],
                                             ROWS[:, 4096 * i + 128 * m:4096 * i + 128 * m + 128]) for m in range(32)])

            def turn(name, l, pieces):
                begin(name, l)
                pe.sem_inc(turns, 1)
                for out, src in pieces:
                    op = nc.tensor.transpose(out, src, IDENT[0:src.shape[0], 0:src.shape[0]])
                op.then_inc(job_done, 1)

            pe.wait_ge(consts_in, 32)
            pe.wait_ge(inputs_in, 80)
            turn("c", 0, [(bank("c")[:, 9 * k:9 * k + 9], CIN[0:9, 128 * k:128 * k + 128]) for k in range(KC)])
            for t, (_, n) in enumerate(tiles):
                for k in range(4):
                    b = bank(f"x{t}_{k}")
                    turn(f"x{t}_{k}", 0, [(b[:, 128 * j:128 * j + n], XIN[0:n, t, 512 * k + 128 * j:512 * k + 128 * j + 128])
                                         for j in range(4)])
            pe.wait_ge(c_ready, 1)

            with pe.Fori(0, DEPTH) as l:
                pe.wait_ge(params_in, l * 272 + 272)
                for i, (r, c) in enumerate(((128, 128), (74, 128), (88, 128), (88, 128), (88, 128), (88, 128), (4, DK))):
                    turn(f"par{i}", l, [(bank(f"par{i}")[0:c, 0:r], STG[0:r, i, 0:c])])
                ones_sum("ss1", l, l * 8)

                with pe.Fori(0, ADA_FIRST // 2) as i:
                    for j in range(2):
                        pe.wait_ge(pair_free[j], pair_value(l, i))
                        for u in range(4):
                            ada_unit(u, u, (l * (UNITS // 4) + i * 2 + (j + 1)) * 16, j)
                mod_turn(l, 0)

                def hn1(k):
                    pe.wait_ge(hn_ready, l * 32 + k)

                with pe.Fori(0, 2) as i:
                    for j in range(2):
                        panel(l, i * 2 + j, 0, j, pair_value(l, Q_QK // 2 + i), HH, HL, ((0, DK), (DK, DK)), ready=hn1)
                for j in range(4):
                    panel(l, 0, G_V + 8 * j, j % 2, pair_value(l, (Q_V + j) // 2), HH, HL)
                begin("glr", l)
                granules(l, 0, G_GLR, 0, 0, HH, HL, ((0, 128),), KC - 1, 8, out=bank("glr"))
                with pe.Fori(0, 8) as i:
                    for j in range(2):
                        panel(l, i * 2 + j, G_REST, j, pair_value(l, Q_REST // 2 + i), HH, HL)

                pe.wait_ge(glr_ready, l + 1)
                for h in range(H):
                    ahead(f"alpha{h}", l)
                    b = begin(f"alpha{h}", l)
                    mm(b[0:DK, 0:T], WAL[:, DK * h:DK * h + DK], TMP[0:RANK, 0, :], True, True).then_inc(job_done, 1)
                pe.wait_ge(z_ready, l + 1)
                for t, (tok, n) in enumerate(tiles):
                    for k in range(2):
                        ahead(f"vt{t}_{k}", l)
                        b = bank(f"vt{t}_{k}")
                        turn(f"vt{t}_{k}", l, [(b[0:n, 128 * j:128 * j + 128], Z[:, 8 + 4 * k + j, tok]) for j in range(4 - 2 * k)])
                for h in range(H):
                    s = h % 2
                    for k in range(8):
                        ahead(f"lev{h}_{k}", l)
                        b = begin(f"lev{h}_{k}", l)
                        if k < 7:
                            pe.wait_ge(qk_ready, l * 64 + (16 * h + 2 * k + 2))
                            q, kk = QP[:, k % 2, :], KP[:, k % 2, :]
                        else:
                            q, kk = Z[0:DK, h, :], Z[0:DK, 4 + h, :]
                        for tok, n in (tiles if LEVELS[k] <= 4 else tiles[0:2]):
                            op = mm(b[0:n, tok], kk[:, tok], q[:, tok], True, True)
                        op.then_inc(job_done, 1)
                    ahead(f"kt{h}", l)
                    pe.wait_ge(qk_ready, l * 64 + (16 * h + 16))
                    b = bank(f"kt{h}")
                    turn(f"kt{h}", l, [(b[0:n, DK * t:DK * t + DK], KP[:, 1, tok]) for t, (tok, n) in enumerate(tiles)])
                    ahead(f"kv{h}_0", l)
                    if h == 0:
                        pe.wait_ge(v_ready, l * 2 + 1)
                    v0 = DV * h
                    pe.wait_ge(ktm_ready, l * 8 + (h + 1))
                    b = begin(f"kv{h}_0", l)
                    mm(b[0:DK, 0:DV], KTM[:, 0, :], VTM[:, 0, v0:v0 + DV], True, True).then_inc(job_done, 1)
                    pe.wait_ge(att_ready, l * 8 + (h + 1))
                    pe.wait_ge(s1_ready, l * 8 + (h + 1))
                    pe.wait_ge(state_in, l * 128 + 16 * (h + 1))
                    for i, (_, r0, m, c) in enumerate(gla_segments(h)):
                        ahead(f"o{h}_{i}", l)
                        b = begin(f"o{h}_{i}", l)[r0:r0 + m]
                        v = slice(v0 + c, v0 + c + m)
                        mm(b[:, 0:128], VTM[:, 0, v], ATT[:, s, 0:128], True, True)
                        mm(b[:, 128:256], VTM[:, 1, v], ATT[:, s, 128:256], True, False)
                        mm(b[:, 128:256], ST[:, 8, c:c + m], QP[:, 1, 128:256], False, True)
                        mm(b[:, 256:320], VTM[0:64, 2, v], ATT[0:64, s, 256:320], True, True)
                        for e in range(NS):
                            tok = slice(SEQ + TS * e, SEQ + TS * e + TS)
                            op = more(b[:, tok], ST[:, e, c:c + m], QP[:, 1, tok])
                        op.then_inc(job_done, 1)
                    ahead(f"kv{h}_1", l)
                    b = begin(f"kv{h}_1", l)
                    mm(b[0:DK, 0:DV], KTM[:, 1, :], VTM[:, 1, v0:v0 + DV], True, True).then_inc(job_done, 1)
                    pe.wait_ge(ktmm_ready, l * 8 + (h + 1))
                    for i in range(4):
                        ahead(f"kvs{h}_{i}", l)
                        b = begin(f"kvs{h}_{i}", l)
                        for j in range(2):
                            op = mm(b[0:DK, DV * j:DV * j + DV], KTMM[:, 2 * i + j, :], VTM[0:64, 2, v0:v0 + DV], True, True)
                        op.then_inc(job_done, 1)
                ahead("hs", l)
                b = begin("hs", l)
                pe.wait_ge(osq_ready, l * 2 + 1)
                for j in range(6):
                    op = mm(b[0:H, 0:T], HIND[:, j, :], Z[:, j, :], j == 0, j == 5)
                op.then_inc(job_done, 1)
                pe.wait_ge(hrs_ready, l * 2 + 1)
                for j in range(6):
                    ahead(f"bc{j}", l)
                    b = begin(f"bc{j}", l)
                    h = j // 3 * 2
                    halves = ((h, 0, 64), (h + 1, 64, 64)) if j % 3 == 1 else ((h + j % 3 // 2, 0, 128),)
                    for hh, r, w in halves:
                        op = mm(b[r:r + w, 0:T], IDENT[0:H, hh:hh + 1].broadcast_to([H, w]), TMP[0:H, 0, :], True, True)
                    op.then_inc(job_done, 1)

                ahead("lcv", l)
                pe.wait_ge(lru_in, l * 224 + 224)
                b = bank("lcv")
                turn("lcv", l, [(b[:, 24 * j:24 * j + 24], SLC[:, 128 * j:128 * j + 128]) for j in range(6)]
                     + [(b[:, 144 + 8 * j:152 + 8 * j], SLH[:, 128 * j:128 * j + 128]) for j in range(6)])
                pe.wait_ge(lco_ready, l + 1)
                for k in range(2):
                    ahead(f"lco{k}", l)
                    b = bank(f"lco{k}")
                    turn(f"lco{k}", l, [(b[0:27, 128 * j:128 * j + 128], LCO[:, 4 * k + j, :]) for j in range(4 - 2 * k)])
                pe.wait_ge(xc_ready, l + 1)
                for j in range(6):
                    q, m = j // 3 * 3, j % 3
                    for g in range(2):
                        ahead(f"gate{g}_{j}", l)
                        b = begin(f"gate{g}_{j}", l)
                        parts = (((0, 0, 0, 128), (1, 0, 96, 32)), ((1, 32, 0, 128), (0, 128, 0, 64), (2, 0, 64, 64)),
                                 ((2, 64, 0, 128), (1, 160, 0, 32)))[m]
                        for i, (k, c, r, w) in enumerate(parts):
                            args = b[r:r + w, 0:T], GW[g][:, q + k, c:c + w], XC[:, q + k, :]
                            op = more(*args) if i else mm(*args, True, True)
                        op.then_inc(job_done, 1)
                pe.wait_ge(lho_ready, l + 1)
                for k in range(2):
                    ahead(f"lho{k}", l)
                    b = bank(f"lho{k}")
                    turn(f"lho{k}", l, [(b[0:9, 128 * j:128 * j + 128], LHO[:, 4 * k + j, :]) for j in range(4 - 2 * k)])

                for t, (tok, n) in enumerate(tiles):
                    ahead(f"rvt{t}", l)
                    b = bank(f"rvt{t}")
                    turn(f"rvt{t}", l, [(b[0:n, 128 * j:128 * j + 128], Z[:, 40 + j, tok]) for j in range(4)])
                pe.wait_ge(rope_done, l * 2 + 2)
                for h in range(H):
                    s = h % 2
                    q, k, v = Z[:, 32 + h, :], Z[:, 36 + h, :], slice(DR * h, DR * h + DR)
                    ahead(f"rqk{h}", l)
                    b = begin(f"rqk{h}", l)
                    for tok, n in tiles:
                        op = mm(b[0:n, tok], k[:, tok], q[:, tok], True, True)
                    op.then_inc(job_done, 1)
                    ahead(f"rkt{h}", l)
                    b = bank(f"rkt{h}")
                    turn(f"rkt{h}", l, [(b[0:n, DR * t:DR * t + DR], k[:, tok]) for t, (tok, n) in enumerate(tiles)])
                    ahead(f"rkv{h}_0", l)
                    if h == 0:
                        pe.wait_ge(v_ready, l * 2 + 2)
                    pe.wait_ge(ktm_ready, l * 8 + (h + 5))
                    b = begin(f"rkv{h}_0", l)
                    mm(b[:, 0:DR], RKT[:, 0, :], RVT[:, 0, v], True, True).then_inc(job_done, 1)
                    ahead(f"ro{h}", l)
                    pe.wait_ge(att_ready, l * 8 + (h + 5))
                    pe.wait_ge(s1_ready, l * 8 + (h + 5))
                    pe.wait_ge(state_in, l * 128 + 16 * (h + 5))
                    b = begin(f"ro{h}", l)
                    mm(b[:, 0:128], RVT[:, 0, v], RAT[:, s, 0:128], True, True)
                    mm(b[:, 128:256], RVT[:, 1, v], RAT[:, s, 128:256], True, False)
                    mm(b[:, 128:256], RST[:, 8, :], RQE[:, s, 128:256], False, True)
                    mm(b[:, 256:320], RVT[0:64, 2, v], RAT[0:64, s, 256:320], True, True)
                    for e in range(NS):
                        tok = slice(SEQ + TS * e, SEQ + TS * e + TS)
                        op = more(b[:, tok], RST[:, e, :], RQE[:, s, tok])
                    op.then_inc(job_done, 1)
                    ahead(f"rkv{h}_1", l)
                    b = begin(f"rkv{h}_1", l)
                    mm(b[:, 0:DR], RKT[:, 1, :], RVT[:, 1, v], True, True).then_inc(job_done, 1)
                    pe.wait_ge(ktmm_ready, l * 8 + (h + 5))
                    for i in range(2):
                        ahead(f"rkvs{h}_{i}", l)
                        b = begin(f"rkvs{h}_{i}", l)
                        for j in range(4):
                            op = mm(b[:, DR * j:DR * j + DR], RKM[:, 4 * i + j, :], RVT[0:64, 2, v], True, True)
                        op.then_inc(job_done, 1)
                ahead("rhs", l)
                b = begin("rhs", l)
                pe.wait_ge(osq_ready, l * 2 + 2)
                for j in range(4):
                    op = mm(b[0:H, 0:T], RIND[:, j, :], Z[:, 36 + j, :], j == 0, j == 3)
                op.then_inc(job_done, 1)
                pe.wait_ge(hrs_ready, l * 2 + 2)
                for j in range(4):
                    ahead(f"rbc{j}", l)
                    b = begin(f"rbc{j}", l)
                    mm(b[:, 0:T], IDENT[0:H, j:j + 1].broadcast_to([H, 128]), TMP[0:H, 0, :], True, True).then_inc(job_done, 1)

                mod_turn(l, 1)

                pe.wait_ge(mix_ready, l * 3 + 3)
                job = 0
                for q in range(8):
                    panel(l, 0, G_OUT + 8 * q, q % 2, pair_value(l, (Q_OUT + q) // 2), MH, ML)
                    if q == 0:
                        pe.wait_ge(hist_in, l * 16 + 16)
                    for _ in range(3 if q < 6 else 2):
                        b = bank(f"hist{job}")
                        turn(f"hist{job}", l, [(b[:, 16 * j:16 * j + 16], STF[:, 512 * job + 128 * j:512 * job + 128 * j + 128])
                                               for j in range(4)])
                        job += 1
                ones_sum("ss2", l, l * 8 + 4)

                def hn2(k):
                    pe.wait_ge(hn_ready, l * 32 + (16 + k))

                first = 0
                for p, (n, k) in enumerate(zip(PARTS, DOWN_K)):
                    with pe.Fori(0, n) as i:
                        for side in range(2):
                            panel(l, i * 2 + side, G_UP[p], side, pair_value(l, Q_UP[p] // 2 + i), HH, HL,
                                  ready=hn2 if p == 0 else None)
                    first += n

                    def hidden(k):
                        pe.wait_ge(hid_ready, l * 22 + (first - n + k // 2))

                    if k == 4:
                        with pe.Fori(0, 4) as i:
                            for j in range(2):
                                panel(l, i * 2 + j, G_DOWN[p], j, pair_value(l, Q_DOWN[p] // 2 + i), MH, ML, ready=hidden)
                    else:
                        job = 0
                        for q in range(8):
                            panel(l, 0, G_DOWN[p] + 6 * q, q % 2, pair_value(l, (Q_DOWN[p] + q) // 2), MH, ML, n=6, ready=hidden)
                            for _ in range(3 if q < 6 else 2):
                                b = bank(f"xo{job}")
                                turn(f"xo{job}", l, [(b[0:18, 128 * j:128 * j + 128], XO[:, 4 * job + j, :]) for j in range(4)])
                                job += 1

            ones_sum("ssf", 0, DEPTH * 8)
            pe.wait_ge(hn_f32, DEPTH * 32 + KC)
            for t, (tok, n) in enumerate(tiles):
                for k in range(4):
                    b = bank(f"y{t}_{k}")
                    turn(f"y{t}_{k}", 0, [(b[0:n, 128 * j:128 * j + 128], SQ[:, 4 * k + j, tok]) for j in range(4)])


INS = ["x_prompt", "x_sample", "state_gla", "state_ret", "state_lru", "state_lru_conv", "state_ffn_conv", "c_prompt",
       "c_sample", "norm1_g", "norm2_g", "final_g", "w_ada", "b_ada", "w_in", "gla_w_alpha", "gla_b_alpha", "gla_norm_g",
       "lru_conv_w", "lru_conv_b", "lru_w_a", "lru_b_a", "lru_w_x", "lru_b_x", "lru_lambda", "ret_norm_g", "w_out",
       "ffn_w_up", "ffn_conv_w", "ffn_conv_b", "ffn_w_down"]
PAST = 2048
OUTS = [("y_p", (1, SEQ, D)), ("y_s", (NS, TS, D))]
for _s, _b in (("p", 1), ("s", NS)):
    OUTS += [(f"gla_{_s}", (DEPTH, _b, H, DK, DV)), (f"ret_{_s}", (DEPTH, _b, H, DR, DR)), (f"lru_{_s}", (DEPTH, _b, W3)),
             (f"lconv_{_s}", (DEPTH, _b, 3, W3)), (f"fconv_{_s}", (DEPTH, _b, 2, 2 * D_FF))]


def constants():
    import numpy as np
    cst = np.zeros((P, 304), np.float32)
    cst[:, 0:128] = np.eye(P)
    cst[:, 128:256] = 1.0
    for j in range(6):
        for r in range(P):
            cst[r, 256 + 4 * j + (128 * j + r) // DV] = 1.0
    for j in range(4):
        cst[:, 280 + 5 * j] = 1.0
    for r in range(64):
        cst[r, 296 + r // TS] = 1.0
    keep = np.ones((P, T), np.float32)
    keep[:, [0, 128] + [SEQ + TS * b for b in range(NS)]] = 0.0
    masks = np.zeros((P, 8, 192), np.float32)
    for k, hs in enumerate(LEVELS):
        for n, c0 in ((128, 0), (64, 128)):
            s, t = np.arange(n)[:, None], np.arange(n)[None, :]
            if hs == 0:
                m = s == t
            else:
                m = (s // (2 * hs) == t // (2 * hs)) & (s % (2 * hs) < hs) & (t % (2 * hs) >= hs)
                if n == 64 and hs > 4:
                    m = m & False
            masks[0:n, k, c0:c0 + n] = m
    pos = np.concatenate([np.arange(SEQ), PAST + np.tile(np.arange(TS), NS)]).astype(np.float32)
    half = DR // 2
    freqs = np.float32(10000.0) ** (-np.arange(half, dtype=np.float32) / np.float32(half))
    ang = freqs[:, None] * pos[None, :]
    cos, sin = np.cos(ang).astype(np.float32), np.sin(ang).astype(np.float32)
    rd = np.zeros((P, H, 192), np.float32)
    qd = np.zeros((P, H, T), np.float32)
    kd = np.ones((P, 2, H), np.float32)
    local = np.concatenate([np.arange(SEQ) % 128, np.tile(np.arange(TS), NS)])
    for h in range(H):
        lg = np.log1p(-np.exp2(-5.0 - h))
        for n, c0 in ((128, 0), (64, 128)):
            s, t = np.arange(n)[:, None], np.arange(n)[None, :]
            ok = (s <= t) & ((s // TS == t // TS) | (n == 128))
            rd[0:n, h, c0:c0 + n] = np.where(ok, np.exp(np.maximum(t - s, 0) * lg) * DR ** -0.5, 0.0)
        qd[:, h, :] = np.exp((local + 1) * lg) * DR ** -0.5
        kd[:, 0, h] = np.exp((127 - np.arange(P)) * lg)
        kd[:, 1, h] = np.exp((TS - 1 - np.arange(P) % TS) * lg)
    return {"k_cst": cst, "k_keep": keep, "k_masks": masks, "k_cos": np.concatenate([cos, cos]),
            "k_sin": np.concatenate([-sin, sin]), "k_rd": rd, "k_qd": qd, "k_kd": kd}


def kernel(**inputs):
    import numpy as np
    import concourse.bacc as bacc
    from concourse.bass_utils import run_bass_kernel_spmd as run

    nc = bacc.Bacc("TRN2", target_bir_lowering=False, num_devices=1)
    arrays = {n: np.ascontiguousarray(inputs[n]) for n in INS}
    arrays.update(constants())
    I = {n: nc.dram_tensor(f"in_{n}", a.shape, mybir.dt.from_np(a.dtype), kind="ExternalInput").ap() for n, a in arrays.items()}
    O = {n: nc.dram_tensor(f"out_{n}", s, mybir.dt.float32, kind="ExternalOutput").ap() for n, s in OUTS}
    build(nc, I, O)
    r = run(nc, [{f"in_{n}": a for n, a in arrays.items()}], core_ids=[0])
    return tuple(r.results[0][f"out_{n}"] for n, _ in OUTS)
```
